# Optimizing a Trainium2 kernel written in Bass

```python
import jax, jax.numpy as jnp
from jax import lax
import numpy as np

D_MODEL = 1024
BATCH = 1
SEQ = 512
DEPTH = 1

PLE_DIM = 256
RET_HEADS = 4
RET_QK_DIM = 128
RET_V_DIM = 256
RET_QK_WIDTH = RET_HEADS * RET_QK_DIM
RET_V_WIDTH = RET_HEADS * RET_V_DIM
RET_CHUNK = 128
ROPE_BASE = 10000.0
CONV_CH = D_MODEL
CONV_WIDTH = 31
N_EXPERTS = 32
TOP_K = 4
D_FF = D_MODEL
SWIGLU_LIMIT = 7.0
SWIGLU_ALPHA = 1.702
MOE_BLOCK = 128
EPS = 1e-6
IN_WIDTHS = (RET_QK_WIDTH, RET_QK_WIDTH, RET_V_WIDTH, RET_V_WIDTH, CONV_CH, CONV_CH, D_MODEL, D_MODEL)
IN_WIDTH = 2 * RET_QK_WIDTH + 2 * RET_V_WIDTH + 2 * CONV_CH + 2 * D_MODEL

kernel_name = "hybrid_retention_conformer_moe_block"

def rms_norm(x, g):
    xf = x.astype(jnp.float32)
    y = xf * lax.rsqrt(jnp.mean(xf * xf, axis=-1, keepdims=True) + EPS)
    return (y * g.astype(jnp.float32)).astype(x.dtype)

def layer_norm(x, g, b):
    xf = x.astype(jnp.float32)
    mu = jnp.mean(xf, axis=-1, keepdims=True)
    var = jnp.mean(jnp.square(xf - mu), axis=-1, keepdims=True)
    y = (xf - mu) * lax.rsqrt(var + EPS)
    return (y * g.astype(jnp.float32) + b.astype(jnp.float32)).astype(x.dtype)

def rotary(t, pos):
    half = t.shape[-1] // 2
    inv_freq = ROPE_BASE ** (-jnp.arange(half, dtype=jnp.float32) / half)
    ang = pos[:, None] * inv_freq[None, :]
    cos = jnp.cos(ang)[None, :, None, :].astype(t.dtype)
    sin = jnp.sin(ang)[None, :, None, :].astype(t.dtype)
    t1, t2 = t[..., :half], t[..., half:]
    return jnp.concatenate([t1 * cos - t2 * sin, t2 * cos + t1 * sin], axis=-1)

def retention_chunkwise(q, k, v):
    b, s, h, dk = q.shape
    dv = v.shape[-1]
    c = RET_CHUNK
    n = s // c
    log_gamma = jnp.log1p(-jnp.exp2(-5.0 - jnp.arange(h, dtype=jnp.float32)))
    idx = jnp.arange(c, dtype=jnp.float32)
    rel = idx[:, None] - idx[None, :]
    decay_in = jnp.where(rel >= 0, jnp.exp(log_gamma[:, None, None] * jnp.maximum(rel, 0.0)), 0.0)
    decay_q = jnp.exp(log_gamma[:, None] * (idx + 1.0))[None, :, :, None]
    decay_k = jnp.exp(log_gamma[:, None] * (c - 1.0 - idx))[None, :, :, None]
    decay_chunk = jnp.exp(log_gamma * c)[None, :, None, None]

    def to_chunks(t):
        return t.reshape(b, n, c, h, t.shape[-1]).transpose(1, 0, 3, 2, 4)

    qc, kc, vc = to_chunks(q), to_chunks(k), to_chunks(v)

    def step(state, inp):
        qi, ki, vi = inp
        scores = jnp.einsum('bhid,bhjd->bhij', qi, ki) * decay_in
        inner = jnp.einsum('bhij,bhje->bhie', scores, vi)
        cross = jnp.einsum('bhid,bhde->bhie', qi, state) * decay_q
        state = state * decay_chunk + jnp.einsum('bhjd,bhje->bhde', ki * decay_k, vi)
        return state, inner + cross

    state0 = jnp.zeros((b, h, dk, dv), jnp.float32)
    _, out = lax.scan(step, state0, (qc, kc, vc))
    return out.transpose(1, 0, 3, 2, 4).reshape(b, s, h, dv)

def head_group_norm(o, g):
    mu = jnp.mean(o, axis=-1, keepdims=True)
    var = jnp.mean(jnp.square(o - mu), axis=-1, keepdims=True)
    y = (o - mu) * lax.rsqrt(var + EPS)
    b, s = o.shape[0], o.shape[1]
    return y.reshape(b, s, RET_V_WIDTH) * g.astype(jnp.float32)

def causal_depthwise_conv(u, w, bias):
    out = lax.conv_general_dilated(
        u, w[:, None, :].astype(u.dtype), window_strides=(1,),
        padding=((CONV_WIDTH - 1, 0),),
        dimension_numbers=('NWC', 'WIO', 'NWC'),
        feature_group_count=u.shape[-1])
    return out + bias

def moe(h, w_router, b_router, w_gu, b_gu, w_down, b_down):
    b, s, d = h.shape
    t = b * s
    hf = h.reshape(t, d)
    logits = (hf @ w_router + b_router).astype(jnp.float32)
    top_logit, top_idx = lax.top_k(logits, TOP_K)
    top_w = jax.nn.softmax(top_logit, axis=-1)
    n_assign = t * TOP_K
    flat_e = top_idx.reshape(-1)
    flat_w = top_w.reshape(-1)
    flat_tok = jnp.repeat(jnp.arange(t, dtype=jnp.int32), TOP_K)
    order = jnp.argsort(flat_e)
    sorted_e = flat_e[order]
    counts = jnp.bincount(flat_e, length=N_EXPERTS)
    padded = ((counts + MOE_BLOCK - 1) // MOE_BLOCK) * MOE_BLOCK
    start = jnp.cumsum(counts) - counts
    pend = jnp.cumsum(padded)
    pstart = pend - padded
    dest = pstart[sorted_e] + (jnp.arange(n_assign, dtype=jnp.int32) - start[sorted_e])
    cap = n_assign + N_EXPERTS * MOE_BLOCK
    n_blocks = cap // MOE_BLOCK
    buf_tok = jnp.zeros((cap,), jnp.int32).at[dest].set(flat_tok[order])
    buf_w = jnp.zeros((cap,), jnp.float32).at[dest].set(flat_w[order])
    block_e = jnp.minimum(
        jnp.searchsorted(pend, jnp.arange(n_blocks, dtype=pend.dtype) * MOE_BLOCK, side='right'),
        N_EXPERTS - 1)
    xb = hf[buf_tok].reshape(n_blocks, MOE_BLOCK, d)

    def expert_block(args):
        xe, e = args
        gu = xe @ w_gu[e] + b_gu[e]
        gate, up = gu[:, :D_FF], gu[:, D_FF:]
        gate = jnp.minimum(gate, SWIGLU_LIMIT)
        up = jnp.clip(up, -SWIGLU_LIMIT, SWIGLU_LIMIT)
        act = (up + 1.0) * gate * jax.nn.sigmoid(SWIGLU_ALPHA * gate)
        return act @ w_down[e] + b_down[e]

    yb = lax.map(expert_block, (xb, block_e)).reshape(cap, d)
    y = jax.ops.segment_sum(yb * buf_w[:, None].astype(yb.dtype), buf_tok, num_segments=t)
    return y.reshape(b, s, d)

def setup_inputs(seed: int = 0) -> dict:
    key = jax.random.key(seed)
    ks = jax.random.split(key, 24)
    f32 = jnp.float32
    L, D = DEPTH, D_MODEL

    def nrm(k, shape, fan_in):
        return jax.random.normal(k, shape, f32) * (fan_in ** -0.5)

    def gain(k, shape):
        return 1.0 + 0.02 * jax.random.normal(k, shape, f32)

    def small(k, shape):
        return 0.01 * jax.random.normal(k, shape, f32)

    return {
        "x": jax.random.normal(ks[0], (BATCH, SEQ, D), f32),
        "p": jax.random.normal(ks[1], (DEPTH, BATCH, SEQ, PLE_DIM), f32),
        "g_mix": gain(ks[2], (L, D)),
        "w_in": nrm(ks[3], (L, D, IN_WIDTH), D),
        "ret_gn_w": gain(ks[4], (L, RET_V_WIDTH)),
        "w_ret_out": nrm(ks[5], (L, RET_V_WIDTH, D), RET_V_WIDTH),
        "w_dw": nrm(ks[6], (L, CONV_WIDTH, CONV_CH), CONV_WIDTH),
        "b_dw": small(ks[7], (L, CONV_CH)),
        "conv_ln_w": gain(ks[8], (L, CONV_CH)),
        "conv_ln_b": small(ks[9], (L, CONV_CH)),
        "w_conv_out": nrm(ks[10], (L, CONV_CH, D), CONV_CH),
        "b_conv_out": small(ks[11], (L, D)),
        "w_o": nrm(ks[12], (L, D, D), D),
        "g_ffn": gain(ks[13], (L, D)),
        "w_router": nrm(ks[14], (L, D, N_EXPERTS), D),
        "b_router": small(ks[15], (L, N_EXPERTS)),
        "w_gu": nrm(ks[16], (L, N_EXPERTS, D, 2 * D_FF), D),
        "b_gu": small(ks[17], (L, N_EXPERTS, 2 * D_FF)),
        "w_down": nrm(ks[18], (L, N_EXPERTS, D_FF, D), D_FF),
        "b_down": small(ks[19], (L, N_EXPERTS, D)),
        "g_ple": gain(ks[20], (L, D)),
        "w_ple_gate": nrm(ks[21], (L, D, D), D),
        "w_ple_proj": nrm(ks[22], (L, PLE_DIM, D), PLE_DIM),
        "g_final": gain(ks[23], (D,)),
    }

def reference(x, p, g_mix, w_in, ret_gn_w, w_ret_out, w_dw, b_dw, conv_ln_w, conv_ln_b,
              w_conv_out, b_conv_out, w_o, g_ffn, w_router, b_router, w_gu, b_gu,
              w_down, b_down, g_ple, w_ple_gate, w_ple_proj, g_final):
    b, s, _ = x.shape
    pos = jnp.arange(s, dtype=jnp.float32)
    splits = np.cumsum(IN_WIDTHS)[:-1].tolist()
    for i in range(DEPTH):
        h = rms_norm(x, g_mix[i])
        u = h @ w_in[i]
        q, k, v, g_ret, glu_a, glu_b, m_ret, m_conv = jnp.split(u, splits, axis=-1)

        q = rotary(q.reshape(b, s, RET_HEADS, RET_QK_DIM), pos)
        k = rotary(k.reshape(b, s, RET_HEADS, RET_QK_DIM), pos) * (RET_QK_DIM ** -0.5)
        v = v.reshape(b, s, RET_HEADS, RET_V_DIM)
        ret = retention_chunkwise(q.astype(jnp.float32), k.astype(jnp.float32), v.astype(jnp.float32))
        ret = head_group_norm(ret, ret_gn_w[i]).astype(x.dtype)
        y_ret = (jax.nn.silu(g_ret) * ret) @ w_ret_out[i]

        c = glu_a * jax.nn.sigmoid(glu_b)
        c = causal_depthwise_conv(c, w_dw[i], b_dw[i])
        c = jax.nn.silu(layer_norm(c, conv_ln_w[i], conv_ln_b[i]))
        y_conv = c @ w_conv_out[i] + b_conv_out[i]

        mixed = jax.nn.sigmoid(m_ret) * y_ret + jax.nn.sigmoid(m_conv) * y_conv
        x = x + mixed @ w_o[i]

        x = x + moe(rms_norm(x, g_ffn[i]), w_router[i], b_router[i], w_gu[i], b_gu[i],
                    w_down[i], b_down[i])

        gate = jax.nn.sigmoid(rms_norm(x, g_ple[i]) @ w_ple_gate[i])
        x = x + gate * (p[i] @ w_ple_proj[i])
    return rms_norm(x, g_final)


_drawn_inputs = setup_inputs


def setup_inputs(seed=0):
    import zlib

    import numpy as np

    out = dict(_drawn_inputs(seed))
    spreads = {}
    factors = {'ret_gn_w': 2.815,
     'conv_ln_b': 3.869,
     'b_gu': 8.0,
     'b_down': 8.0,
     'g_ple': 140.208,
     'g_final': 24.608,
     'b_dw': 3.156,
     'b_conv_out': 2.849}
    for name, (base, spread) in spreads.items():
        noise = np.random.default_rng([zlib.crc32(name.encode()), seed]).standard_normal(out[name].shape)
        drawn = base * np.exp(spread * noise) if base else spread * noise
        out[name] = __import__('jax').numpy.asarray(drawn.astype(out[name].dtype))
    for name, factor in factors.items():
        out[name] = (out[name] * factor).astype(out[name].dtype)
    return out
```

```python
from contextlib import ExitStack

import concourse.bass as bass
from concourse import mybir
from concourse.alu_op_type import AluOpType as ALU

F32 = mybir.dt.float32
F32R = mybir.dt.float32r
I32 = mybir.dt.int32
U32 = mybir.dt.uint32
ACT = mybir.ActivationFunctionType
AX_X = mybir.AxisListType.X

P = 128
T = 512
D = 1024
TT = T // P
CT = D // P
NCOL = 512
HEADS, DK, DV = 4, 128, 256
HALF = DK // 2
TAPS = 31
NE, TOPK = 32, 4
FF = 1024
PLE = 256
LIMIT, ALPHA = 7.0, 1.702
EPS = 1e-6
CAP = 96
PASSES = -(-T // CAP)
EMPTY = 4096
SLOTS = 12
GU_SLOTS = 8

COL_Q, COL_K, COL_V, COL_G = 0, 512, 1024, 2048
COL_GLU_A, COL_GLU_B, COL_MRET, COL_MCONV = 3072, 4096, 5120, 6144

CH_GLU, CH_QK, CH_V, CH_G, CH_MC, CH_MR, CH_YR, CH_YC, CH_WO, CHUNKS = 0, 4, 6, 8, 10, 12, 14, 16, 18, 20
CHUNK_DECAY = [(1.0 - 2.0 ** (-5 - h)) ** P for h in range(HEADS)]
DVE_PAIRS, POOL_PAIR = (0, 2, 3), 1
CONV_STEPS = {3: 6, 4: 5, 5: 6, 6: 5, 7: 6, 8: 6, 9: 5, 10: 6}
CONV_START = 6

TAP_ROWS = TAPS * CT // 2

PR_MIX, PR_GN, PR_BDW, PR_LNW, PR_LNB, PR_BCO, PR_FFN, PR_PLE = (8 * i for i in range(8))


class Chain:

    def __init__(self, eng, sem, base=0):
        self.eng, self.sem, self.base, self.n = eng, sem, base, 0

    def mark(self, ins):
        ins.then_inc(self.sem, 1)
        self.n += 1
        return self.n

    def wait(self, n):
        self.eng.wait_ge(self.sem, self.base + n)

    def link(self, ins):
        self.wait(self.mark(ins))


def build_layer(nc, t):
    with ExitStack() as ctx:
        base = -(-nc.sbuf_base // 64) * 64

        def at(name, kb, shape, dt=F32):
            return nc.alloc_sbuf_tensor_at(name, shape, dt, offset=base + int(kb * 1024))

        def sem(name):
            return ctx.enter_context(nc.semaphore(name))

        bank = [ctx.enter_context(nc.psum_tensor(f"bank{i}", [P, 512], F32)) for i in range(8)]

        x = at("x", 0, [P, TT, D])
        ident = at("ident", 16, [P, P])
        par = at("par", 16.5, [P, 64])
        wdw = at("wdw", 16.75, [P, 2, TAP_ROWS])
        bexp = at("bexp", 17.75, [P, NE, 16])
        w_rout = at("w_rout", 20.75, [P, CT, NE])
        b_rout = at("b_rout", 21.75, [P, NE])
        small = at("small", 21.875, [P, 48])
        ss = small[:, 0:8]
        rank = small[:, 8:24].rearrange("p (t k) -> p t k", k=TOPK)
        wtop = small[:, 24:40].rearrange("p (t k) -> p t k", k=TOPK)
        wsum = small[:, 40:44]
        nmax = small[:, 44:48]
        maxc = at("maxc", 22.0625, [1, 1], I32)
        ones = at("ones", 22.125, [P, P])
        tri = at("tri", 22.625, [P, P])
        cst = at("cst", 23.125, [P, 168])
        iota_cap, iota_e = cst[:, 0:CAP], cst[:, 96:128]
        ids = cst[:, 128:160].rearrange("p (w t k) -> p w t k", w=2, k=TOPK)
        dk_col, eps = cst[:, 160:164], cst[:, 164:165]
        tok_tab = at("tok_tab", 23.8125, [P, NE + 1], U32)
        asg_tab = at("asg_tab", 23.96875, [P, NE + 1], U32)
        idx_g = at("idx_g", 24.125, [P, 1], U32)
        idx_s = at("idx_s", 24.15625, [P, 1], U32)
        M = 24.1875
        raw = [at(f"raw{s}", M + 4 * s, [P, 2, NCOL]) for s in range(4)]
        whi = [at(f"whi{s}", M + 16 + 4 * s, [P, 2, NCOL], F32R) for s in range(4)]
        wlo = [at(f"wlo{s}", M + 32 + 4 * s, [P, 2, NCOL], F32R) for s in range(4)]
        h_hi = at("h_hi", M + 48, [P, CT, T], F32R)
        h_lo = at("h_lo", M + 64, [P, CT, T], F32R)
        cin = at("cin", M + 80, [P, CT, T + TAPS - 1])
        cv = at("cv", M + 97, [P, CT, T])
        q = at("q", M + 113, [P, TT, HEADS, 2, HALF])
        k = at("k", M + 121, [P, TT, HEADS, 2, HALF])
        v = at("v", M + 129, [P, TT, D])
        g = at("g", M + 145, [P, TT, D])
        xn = at("xn", M + 145, [P, TT, D])
        rows = at("rows", M + 113, [P, 3, P])
        brow = at("brow", M + 117, [NE, 2 * FF])
        R = M + 161
        rope = at("rope", R, [P, 4, TT, HALF])
        dmask = at("dmask", R + 4, [P, HEADS, P])
        dq = at("dq", R + 6, [P, HEADS, P])
        sgb = at("sgb", R + 8, [P, 4, T])
        gs = [at(f"gs{i}", R + 8 + 2 * i, [P, T]) for i in range(2)]
        rot_a = at("rot_a", R + 18, [P, HEADS, 2, HALF])
        rot_b = at("rot_b", R + 20, [P, HEADS, 2, HALF])
        rot_pa = at("rot_pa", R + 12, [P, HEADS, 2, HALF])
        rot_pb = at("rot_pb", R + 14, [P, HEADS, 2, HALF])
        tapped = [at("tapped0", R + 16, [P, T]), at("tapped1", R + 2, [P, T])]
        q_T = at("q_T", R + 8, [P, HEADS, P])
        qd_T = at("qd_T", R + 10, [P, HEADS, P])
        k_T = at("k_T", R + 12, [P, HEADS, P])
        s_T = at("s_T", R + 14, [P, HEADS, P])
        kd = at("kd", R + 16, [P, HEADS, DK])
        state = at("state", R + 18, [P, HEADS, DV])
        bn = at("bn", R + 22, [P, HEADS, 6])
        mv = small[:, 8:40].rearrange("p (t h a) -> p t h a", h=HEADS, a=2)
        sm_c = at("sm_c", M + 80, [P, CT, T])
        sm_r = at("sm_r", R + 4, [P, CT, T])
        r_hi = at("r_hi", M + 113, [P, CT, T], F32R)
        r_lo = at("r_lo", M + 129, [P, CT, T], F32R)
        c_hi = at("c_hi", M + 145, [P, CT, T], F32R)
        c_lo = at("c_lo", M + 97, [P, CT, T], F32R)
        sq = [at(f"sq{i}", R + 2 * i, [P, T]) for i in range(2)]
        lsum = at("lsum", R + 20, [P, T])
        lrs = at("lrs", R + 20, [P, T])
        lsg = [at(f"lsg{i}", R + 2 * i, [P, T]) for i in range(2)]
        mx_hi = at("mx_hi", M + 113, [P, CT, T], F32R)
        mx_lo = at("mx_lo", M + 129, [P, CT, T], F32R)
        xn2 = at("xn2", M + 32, [P, TT, D])
        f_T = at("f_T", M + 113, [P, CT, T])
        p_in = at("p_in", M, [P, TT, PLE])
        wpp = at("wpp", M + 8, [P, 2, D])
        p_T = at("p_T", M + 129, [P, 2, T])
        pp = at("pp", M + 16, [P, TT, D])
        lg = at("lg", R + 20, [P, TT, NE])
        msk = at("msk", R + 20.5, [P, TT, NE])
        top = at("top", R + 21, [P, TT, 8])
        topi = at("topi", R + 21.125, [P, TT, 8], U32)
        topf = at("topf", R + 21.25, [P, TT, TOPK])
        oh = at("oh", M + 142, [P, TT, TOPK, NE])
        prod = at("prod", M + 136, [P, TT, TOPK, NE])
        oha = at("oha", M + 136, [P, TT, TOPK, CAP])
        ohb = at("ohb", M + 161, [P, TT, TOPK, 2, NE])
        wslot = [at(f"wslot{s}", M + kb, [P, 2 * D]) for s, kb in
                 enumerate([48, 56, 64, 72, 80, 88, 97, 105, 145, 153, 165, 173])]
        xg = at("xg", M + 113, [P, D])
        x_T = at("x_T", M + 117, [P, CT, CAP])
        z = [at(f"z{i}", M + 120 + 1.5 * i, [P, 2, 2, CAP]) for i in range(2)]
        sg = [at(f"sg{i}", M + 123 + 0.75 * i, [P, 2, CAP]) for i in range(2)]
        gu = [at(f"gu{i}", M + 124.5 + 0.75 * i, [P, 2, CAP]) for i in range(2)]
        act_T = at("act_T", M + 126, [P, CT, CAP])
        act_lo = at("act_lo", M + 126, [P, CT, CAP], F32R)
        act_hi = at("act_hi", M + 129, [P, CT, CAP], F32R)
        dn_hi = [at(f"dn_hi{r}", M + kb, [P, 2 * D], F32R) for r, kb in enumerate([0, 8, 32, 40])]
        dn_lo = [at(f"dn_lo{r}", M + kb, [P, 2 * D], F32R) for r, kb in enumerate([145, 153, 165, 173])]
        wexp = at("wexp", M + 144, [P, TT, NE])
        yr = at("yr", M + 132, [P, D])
        yb = [at(f"yb{i}", M + kb, [P, TOPK, D]) for i, kb in enumerate([145, 165, 113])]
        pg_raw = [at(f"pg_raw{s}", M + 48 + 8 * s, [P, 2, D]) for s in range(4)]
        pg_lo = [at(f"pg_lo{s}", M + 48 + 8 * s, [P, 2, D], F32R) for s in range(4)]
        pg_hi = [at(f"pg_hi{s}", M + kb, [P, 2, D], F32R) for s, kb in enumerate([80, 88, 97, 105])]
        x_hi = at("x_hi", M, [P, TT, CT, P], F32R)
        x_lo = at("x_lo", M + 32, [P, TT, CT, P], F32R)
        gate = [at(f"gate{i}", M + 129 + 2 * i, [P, NCOL]) for i in range(2)]
        sq_out = at("sq_out", M + 133, [P, D])
        bdn = at("bdn", M + 137, [NE, D])
        wexp_T = at("wexp_T", M + 141, [NE, T])
        g_fin = at("g_fin", M + 161, [P, D])

        hf_rows = nc.dram_tensor("hf_rows", (T, D), F32, kind="Internal").ap()
        y_rows = nc.dram_tensor("y_rows", (T * TOPK, D), F32, kind="Internal").ap()

        x_in = [sem(f"x_in{i}") for i in range(TT)]
        par_in = sem("par_in")
        par_done = sem("par_done")
        par_ready = sem("par_ready")
        sq_own = sem("sq_own")
        rms_ready = sem("rms_ready")
        xn_ready = sem("xn_ready")
        turned = sem("turned")
        turned_hi = sem("turned_hi")
        turned_out = sem("turned_out")
        raw_in = [sem(f"raw_in{s}") for s in range(4)]
        hi_ready = sem("hi_ready")
        lo_ready = sem("lo_ready")
        gran_used = sem("gran_used")
        bank_done = sem("bank_done")
        bank_free = sem("bank_free")
        pad_done = sem("pad_done")
        cv_ready = sem("cv_ready")
        cv_pool_ready = sem("cv_pool_ready")
        ls_ready = sem("ls_ready")
        ln_mean = sem("ln_mean")
        ln_cent = sem("ln_cent")
        ln_sq = sem("ln_sq")
        ln_sq_used = sem("ln_sq_used")
        ln_dev = sem("ln_dev")
        ln_z = sem("ln_z")
        ln_sig = sem("ln_sig")
        ln_val = sem("ln_val")
        ln_hi = sem("ln_hi")
        c_ready = sem("c_ready")
        gs_ready = sem("gs_ready")
        q_ready = sem("q_ready")
        k_ready = sem("k_ready")
        bexp_ready = sem("bexp_ready")
        bexp_done = sem("bexp_done")
        tab_in = sem("tab_in")
        eps_ready = sem("eps_ready")
        qkT_done = sem("qkT_done")
        qT_ready = sem("qT_ready")
        kT_ready = sem("kT_ready")
        sc_done = sem("sc_done")
        sT_ready = sem("sT_ready")
        out_done = sem("out_done")
        out_used = sem("out_used")
        dev_ready = sem("dev_ready")
        gated = sem("gated")
        st_done = sem("st_done")
        state_ready = sem("state_ready")
        mix_ready = sem("mix_ready")
        mix_hi = sem("mix_hi")
        mix_lo = sem("mix_lo")
        hf_out = sem("hf_out")
        lg_done = sem("lg_done")
        lg_ready = sem("lg_ready")
        exp_ready = sem("exp_ready")
        msk_ready = sem("msk_ready")
        rank_done = sem("rank_done")
        maxc_ready = sem("maxc_ready")
        oh_ready = sem("oh_ready")
        tab_done = sem("tab_done")
        tab_ready = sem("tab_ready")
        pass_done = sem("pass_done")
        w_in_s = [sem(f"w_in_s{s}") for s in range(SLOTS)]
        slot_used = sem("slot_used")
        idx_g_done = sem("idx_g_done")
        idx_s_done = sem("idx_s_done")
        gathered = sem("gathered")
        xt_done = sem("xt_done")
        xT_ready = sem("xT_ready")
        gu_done = sem("gu_done")
        z_ready = sem("z_ready")
        sg_ready = sem("sg_ready")
        act_ready = sem("act_ready")
        dn_hi_ready = sem("dn_hi_ready")
        dn_lo_ready = sem("dn_lo_ready")
        act_hi_ready = sem("act_hi_ready")
        act_lo_ready = sem("act_lo_ready")
        y_done = sem("y_done")
        yr_ready = sem("yr_ready")
        scattered = sem("scattered")
        rows_left = sem("rows_left")
        xg_zero = sem("xg_zero")
        moe_done = sem("moe_done")
        wexp_ready = sem("wexp_ready")
        experts_left = sem("experts_left")
        yb_in = [sem(f"yb_in{i}") for i in range(TT)]
        bdn_in = sem("bdn_in")
        wT_done = sem("wT_done")
        wT_ready = sem("wT_ready")
        bias_done = sem("bias_done")
        pg_hi_ready = sem("pg_hi_ready")
        pg_lo_ready = sem("pg_lo_ready")
        g_fin_in = sem("g_fin_in")
        x2_ready = sem("x2_ready")
        tail_in = sem("tail_in")
        pT_done = sem("pT_done")
        pT_ready = sem("pT_ready")
        pp_done = sem("pp_done")
        pp_ready = sem("pp_ready")
        x_turned = sem("x_turned")
        x_hi_ready = sem("x_hi_ready")
        x_lo_ready = sem("x_lo_ready")
        pg_done = sem("pg_done")
        gate_used = sem("gate_used")
        inv_ready = sem("inv_ready")
        xn2_own = sem("xn2_own")
        gate_ready = sem("gate_ready")
        x3_ready = sem("x3_ready")
        fin_ready = sem("fin_ready")
        out_sem = sem("out_sem")
        dve_own = sem("dve_own")
        dve_moe = sem("dve_moe")
        dve_pass = sem("dve_pass")
        pool_own = sem("pool_own")
        sp_waited = sem("sp_waited")
        pool_waited = sem("pool_waited")

        def tap(kk, ct):
            r = kk * CT + ct
            return wdw[:, r // TAP_ROWS, r % TAP_ROWS:r % TAP_ROWS + 1]

        def col(first, ct):
            return par[:, first + ct:first + ct + 1]

        def rotate(engine, own, dst, table, b, a, s, done, queue):
            if b:
                queue.wait_ge(done, b)
            cos, sin = (rope[:, table + i, b, :].unsqueeze(1).unsqueeze(1).to_broadcast([P, HEADS, 2, HALF])
                        for i in range(2))
            own.mark(engine.tensor_tensor(a[:], dst[:, b], cos, ALU.mult))
            own.link(engine.tensor_tensor(s[:], dst[:, b], sin, ALU.mult))
            own.mark(engine.tensor_tensor(dst[:, b, :, 0, :], a[:, :, 0, :], s[:, :, 1, :], ALU.subtract))
            engine.tensor_tensor(dst[:, b, :, 1, :], a[:, :, 1, :], s[:, :, 0, :], ALU.add).then_inc(done, 1)

        w_granules = lambda w: w.rearrange("(s k p) n -> s p k n", k=2, p=P)
        win_g, wret_g, wconv_g, wo_g, wpg_g = map(w_granules, (t.w_in, t.w_ret_out, t.w_conv_out, t.w_o, t.w_ple_gate))
        PAR_DMAS, TAB_DMAS = 11, 8

        K_TURNED = {(10, 3): 0, (12, 1): 2, (13, 0): 3}
        RET_TURNED = {(14, 1): (0, 1), (14, 2): (2, 3), (14, 3): (4, 5, 6, 7)}

        block = ctx.enter_context(nc.Block())

        @block.sync
        def _(sp):
            x_t = t.x.rearrange("(t p) d -> t p d", p=P)
            for i in range(TT):
                sp.dma_start(x[:, i, :], x_t[i]).then_inc(x_in[i], 16)

            def chunk(src, c, column):
                for s in range(4):
                    if not isinstance(c, int) or c > 0:
                        sp.wait_ge(lo_ready, 4 * (c - 1) + s + 1)
                    sp.dma_start(raw[s][:], src[s, :, :, bass.ds(column, NCOL)]).then_inc(raw_in[s], 16)

            sp.wait_ge(par_in, 16 * PAR_DMAS)
            chunk(win_g, 0, COL_GLU_B)
            chunk(win_g, 1, COL_GLU_A)
            chunk(win_g, 2, COL_GLU_B + NCOL)
            chunk(win_g, 3, COL_GLU_A + NCOL)
            with sp.Fori(0, CH_MC - CH_QK) as j:
                chunk(win_g, j + CH_QK, j * NCOL)
            with sp.Fori(0, 2) as j:
                chunk(win_g, j + CH_MC, j * NCOL + COL_MCONV)
            with sp.Fori(0, 2) as j:
                chunk(win_g, j + CH_MR, j * NCOL + COL_MRET)
            for first, src in ((CH_YR, wret_g), (CH_YC, wconv_g), (CH_WO, wo_g)):
                with sp.Fori(0, 2) as j:
                    chunk(src, j + first, j * NCOL)

            gu_w = t.w_gu.rearrange("e (s p) n -> e s p n", p=P)
            dn_w = t.w_down.rearrange("e (s k p) n -> e s p k n", k=2, p=P)

            def load_slot(e, s):
                if s < GU_SLOTS:
                    src = gu_w[bass.ds(e, 1), s].rearrange("o p n -> (o p) n")
                    dst = wslot[s][:]
                else:
                    src = dn_w[bass.ds(e, 1), s - GU_SLOTS].rearrange("o p k n -> (o p) k n")
                    dst = wslot[s][:].rearrange("p (k n) -> p k n", k=2)
                sp.dma_start(dst, src).then_inc(w_in_s[s], 16)

            def load_expert(n, e):
                for s in range(SLOTS):
                    if s == 7:
                        sp.wait_ge(gu_done, 4 * n)
                    elif s == 11:
                        sp.wait_ge(y_done, 2 * n)
                    else:
                        sp.wait_ge(slot_used, 10 * (n - 1) + (s + 1 if s < 7 else s))
                    load_slot(e, s)

            sp.wait_ge(bank_done, 4 * CH_YR)
            for s in range(4):
                load_slot(0, s)
            sp.wait_ge(mix_lo, CT)
            for s in range(4, SLOTS):
                load_slot(0, s)
            sp.wait_ge(lo_ready, 4 * CHUNKS)
            sp.dma_start(p_in[:], t.p.rearrange("(t p) d -> p t d", p=P)).then_inc(tail_in, 16)
            sp.dma_start(wpp[:], t.w_ple_proj.rearrange("(k p) n -> p k n", p=P)).then_inc(tail_in, 16)
            with sp.Fori(1, NE) as e:
                load_expert(e, e)
            sp.wait_ge(gu_done, 4 * NE)
            sp.wait_ge(maxc_ready, 1)
            fullest = sp.value_load(maxc[0:1, 0:1], min_val=0, max_val=T)
            with sp.If(fullest > CAP):
                with sp.Fori(1, PASSES) as m:
                    with sp.If(fullest > m * CAP):
                        with sp.Fori(0, NE) as e:
                            load_expert(m * NE + e, e)
                        sp.wait_ge(gu_done, m * 4 * NE + 4 * NE)
                        sp.sem_inc(sp_waited, 1)

            for s in range(4):
                sp.dma_start(pg_raw[s][:], wpg_g[s]).then_inc(raw_in[s], 16)
            sp.dma_start(bdn[:], t.b_down).then_inc(bdn_in, 16)
            sp.wait_ge(experts_left, 1)
            sp.wait_ge(moe_done, 1)
            y_t = y_rows.rearrange("(t p k) d -> t p k d", p=P, k=TOPK)
            for i in range(TT):
                if i >= 3:
                    sp.wait_ge(x2_ready, i - 2)
                sp.dma_start(yb[i % 3][:], y_t[i]).then_inc(yb_in[i], 16)
            sp.dma_start(g_fin[:], t.g_final.partition_broadcast(P)).then_inc(g_fin_in, 16)
            out_t = t.out.rearrange("(t p) d -> t p d", p=P)
            for i in range(TT):
                sp.wait_ge(fin_ready, i + 1)
                sp.dma_start(out_t[i], x[:, i, :]).then_inc(out_sem, 16)
            sp.wait_ge(out_sem, 16 * TT)

        def pe_chunk(pe, c, hi, lo, stationary, ready=None, after=None):
            for s in range(4):
                pe.wait_ge(lo_ready, 4 * c + s + 1)
                for kk in range(2):
                    kt = 2 * s + kk
                    if ready:
                        ready(kt)
                    for b in range(4):
                        if kt == 0 and (not isinstance(c, int) or c > 0):
                            pe.wait_ge(bank_free, 4 * (c - 1) + b + 1)
                        cols = slice(b * P, (b + 1) * P)
                        for i, (w, o) in enumerate(((whi, hi), (whi, lo), (wlo, hi))):
                            a = w[s][:, kk, cols] if stationary else o[:, kt, cols]
                            m = o[:, kt, :] if stationary else w[s][:, kk, :]
                            mm = nc.tensor.matmul(bank[b][:], a, m, start=(kt == 0 and i == 0),
                                                  stop=(kt == CT - 1 and i == 2))
                        if kt == CT - 1:
                            mm.then_inc(bank_done, 1)
                if s < 3:
                    mm.then_inc(gran_used, 1)
                if after:
                    after(s)

        def turn(pe, i, src, ct):
            if i >= 4:
                pe.wait_ge(turned_out, i - 3)
            for tt in range(TT):
                tr = nc.tensor.transpose(bank[4 + i % 4][:, tt * P:(tt + 1) * P],
                                         src[:, tt, ct * P:(ct + 1) * P], ident[:])
            tr.then_inc(turned, 1)

        @block.tensor
        def _(pe):
            pe.wait_ge(par_in, 16 * PAR_DMAS)
            nc.tensor.transpose(bank[4][:, 0:64], rows[0:64, 0, :], ident[0:64, 0:64])
            for i in range(2):
                tr = nc.tensor.transpose(bank[4][:, 64 + TAP_ROWS * i:64 + TAP_ROWS * (i + 1)],
                                         rows[0:TAP_ROWS, 1 + i, :], ident[0:TAP_ROWS, 0:TAP_ROWS])
            tr.then_inc(par_done, 1)
            pe.wait_ge(par_ready, 1)
            pe.wait_ge(xn_ready, TT)
            for ct in range(CT):
                turn(pe, ct, xn, ct)
            pe_chunk(pe, 0, h_hi, h_lo, True, ready=lambda kt: pe.wait_ge(turned_out, kt + 1))
            pe.wait_ge(tab_in, 16 * TAB_DMAS)
            for i in range(16):
                tr = nc.tensor.transpose(bank[4][:, i * NE:(i + 1) * NE], brow[:, i * P:(i + 1) * P],
                                         ident[0:NE, 0:NE])
            tr.then_inc(bexp_done, 1)
            with pe.Fori(1, CH_QK) as c:
                pe_chunk(pe, c, h_hi, h_lo, True)
            with pe.Fori(CH_QK, CH_MC) as c:
                pe_chunk(pe, c, h_hi, h_lo, False)

            def turn_qk(j):
                if j == 0:
                    pe.wait_ge(q_ready, TT)
                    pe.wait_ge(k_ready, TT)
                    pe.wait_ge(bexp_ready, 1)
                else:
                    pe.wait_ge(out_used, j)
                for h in range(HEADS):
                    nc.tensor.transpose(bank[4][:, h * P:(h + 1) * P],
                                        q[:, j, h].rearrange("p a b -> p (a b)"), ident[:])
                for h in range(HEADS):
                    tr = nc.tensor.transpose(bank[5][:, h * P:(h + 1) * P],
                                             k[:, j, h].rearrange("p a b -> p (a b)"), ident[:])
                tr.then_inc(qkT_done, 1)

            def scores(j):
                pe.wait_ge(qT_ready, j + 1)
                pe.wait_ge(kT_ready, j + 1)
                if j:
                    pe.wait_ge(state_ready, j)
                for h in range(HEADS):
                    mm = nc.tensor.matmul(bank[6][:, h * P:(h + 1) * P], k_T[:, h, :], q_T[:, h, :],
                                          start=True, stop=True)
                mm.then_inc(sc_done, 1)

            def outputs(j):
                pe.wait_ge(sT_ready, j + 1)
                for h in range(HEADS):
                    o = bank[4 + h // 2][:, (h % 2) * DV:(h % 2 + 1) * DV]
                    mm = nc.tensor.matmul(o, s_T[:, h, :], v[:, j, h * DV:(h + 1) * DV], start=True, stop=(j == 0))
                    if j:
                        mm = nc.tensor.matmul(o, qd_T[:, h, :], state[:, h, :], start=False, stop=True)
                mm.then_inc(out_done, 1)
                if j < TT - 1:
                    for h in range(HEADS):
                        mm = nc.tensor.matmul(bank[6 + h // 2][:, (h % 2) * DV:(h % 2 + 1) * DV], kd[:, h, :],
                                              v[:, j, h * DV:(h + 1) * DV], start=True, stop=True)
                    mm.then_inc(st_done, 1)

            steps = {(10, 0): (turn_qk, 0), (10, 1): (scores, 0), (10, 2): (outputs, 0), (10, 3): (turn_qk, 1),
                     (11, 0): (scores, 1), (11, 1): (outputs, 1), (11, 2): (turn_qk, 2), (11, 3): (scores, 2),
                     (12, 0): (outputs, 2), (12, 1): (turn_qk, 3), (12, 2): (scores, 3), (12, 3): (outputs, 3)}

            def retention(c):
                def after(s):
                    if (c, s) in steps:
                        f, j = steps[c, s]
                        f(j)
                return after

            for c in range(CH_MC, CH_MR + 1):
                pe_chunk(pe, c, h_hi, h_lo, True, after=retention(c))

            def turn_ret(s):
                if s == 1:
                    pe.wait_ge(gated, 1)
                for ct in {0: (), 1: (0, 1), 2: (2, 3), 3: (4, 5, 6, 7)}[s]:
                    turn(pe, CT + ct, g, ct)

            pe_chunk(pe, CH_MR + 1, h_hi, h_lo, True, after=turn_ret)

            def layer_norm(c):
                def after(s):
                    if (c, s) == (CH_YR, 0):
                        pe.wait_ge(ls_ready, 1)
                        pe.wait_ge(turned_out, CT + 5)
                        nc.tensor.matmul(bank[4][:], ones[:], lsum[:], start=True, stop=True).then_inc(ln_mean, 1)
                    if (c, s) == (CH_YR, 3):
                        for ct in range(CT):
                            pe.wait_ge(ln_sq, ct + 1)
                            nc.tensor.matmul(bank[5][:], ones[:], sq[ct % 2][:], start=(ct == 0),
                                             stop=(ct == CT - 1)).then_inc(ln_sq_used, 1)
                return after

            pe_chunk(pe, CH_YR, r_hi, r_lo, True, ready=lambda kt: pe.wait_ge(turned_out, CT + kt + 1),
                     after=layer_norm(CH_YR))
            pe_chunk(pe, CH_YR + 1, r_hi, r_lo, True)
            pe_chunk(pe, CH_YC, c_hi, c_lo, True, ready=lambda kt: pe.wait_ge(c_ready, kt + 1))
            pe_chunk(pe, CH_YC + 1, c_hi, c_lo, True)

            def mixed_ready(kt):
                pe.wait_ge(mix_lo, kt + 1)
            pe_chunk(pe, CH_WO, mx_hi, mx_lo, False, ready=mixed_ready)
            pe_chunk(pe, CH_WO + 1, mx_hi, mx_lo, False)

            pe.wait_ge(bank_free, 4 * CHUNKS)
            for ct in range(CT):
                turn(pe, 2 * CT + ct, x, ct)
            pe.wait_ge(tail_in, 32)
            for kt in range(2):
                for tt in range(TT):
                    tr = nc.tensor.transpose(bank[2 + kt][:, tt * P:(tt + 1) * P], p_in[:, tt, kt * P:(kt + 1) * P],
                                             ident[:])
            tr.then_inc(pT_done, 1)
            for tt in range(TT):
                for ct in range(CT):
                    pe.wait_ge(turned_out, 2 * CT + ct + 1) if tt == 0 else None
                    mm = nc.tensor.matmul(bank[0][:, tt * NE:(tt + 1) * NE], f_T[:, ct, tt * P:(tt + 1) * P],
                                          w_rout[:, ct, :], start=(ct == 0), stop=(ct == CT - 1))
            mm.then_inc(lg_done, 1)

            def embed(tiles):
                for i in tiles:
                    tt, n2 = i // 2, i % 2
                    if i >= 2:
                        pe.wait_ge(pp_ready, i - 1)
                    for kt in range(2):
                        mm = nc.tensor.matmul(bank[2 + i % 2][:], p_T[:, kt, tt * P:(tt + 1) * P],
                                              wpp[:, kt, n2 * NCOL:(n2 + 1) * NCOL], start=(kt == 0), stop=(kt == 1))
                    mm.then_inc(pp_done, 1)

            pe.wait_ge(pT_ready, 1)
            embed(range(0, 3))
            pe.wait_ge(msk_ready, 1)
            for tt in range(TT + 1):
                for j in range(min(tt, TT - 1) + 1):
                    mm = nc.tensor.matmul(bank[1][:, tt * NE:(tt + 1) * NE], tri[:] if j == tt else ones[:],
                                          msk[:, j, :], start=(j == 0), stop=(j == min(tt, TT - 1)))
            mm.then_inc(rank_done, 1)
            embed(range(3, 5))

            def turn_x(c):
                pe.wait_ge(gathered, 16 * (c + 1))
                for kt in range(CT):
                    tr = nc.tensor.transpose(bank[6 + kt // 4][:, (kt % 4) * CAP:(kt % 4 + 1) * CAP],
                                             xg[0:CAP, kt * P:(kt + 1) * P], ident[0:CAP, 0:CAP])
                    if kt % 4 == 3:
                        tr.then_inc(xt_done, 1)

            def expert(n, c):
                pe.wait_ge(xT_ready, 2 * c + 2)
                def gate_up(s, b):
                    for i in range(4):
                        mt = 2 * b + i % 2 + CT * (i // 2)
                        mm = nc.tensor.matmul(bank[b][:, i * CAP:(i + 1) * CAP], wslot[s][:, mt * P:(mt + 1) * P],
                                              x_T[:, s, :], start=(s == 0 and i == 0), stop=(s == GU_SLOTS - 1),
                                              skip_group_check=True)
                    return mm

                for s in range(GU_SLOTS - 2):
                    pe.wait_ge(w_in_s[s], 16 * (n + 1))
                    for b in range(4):
                        mm = gate_up(s, b)
                    mm.then_inc(slot_used, 1)
                for s in (GU_SLOTS - 2, GU_SLOTS - 1):
                    pe.wait_ge(w_in_s[s], 16 * (n + 1))
                for b in range(4):
                    mm = gate_up(GU_SLOTS - 2, b)
                    if b == 3:
                        mm.then_inc(slot_used, 1)
                    gate_up(GU_SLOTS - 1, b).then_inc(gu_done, 1)
                turn_x(c + 1)
                pe.wait_ge(yr_ready, 2 * n + 2)
                for r in range(4):
                    pe.wait_ge(dn_lo_ready, 4 * n + r + 1)
                    pe.wait_ge(act_lo_ready, 4 * n + r + 1)
                    for kk in range(2):
                        kt = 2 * r + kk
                        for i, (a, w) in enumerate(((act_hi, dn_hi[r]), (act_hi, dn_lo[r]), (act_lo, dn_hi[r]))):
                            for n2 in range(2):
                                mm = nc.tensor.matmul(bank[4 + n2][0:CAP, :], a[:, kt, :],
                                                      w[:, kk * D + n2 * NCOL:kk * D + (n2 + 1) * NCOL],
                                                      start=(kt == 0 and i == 0), stop=(kt == CT - 1 and i == 2))
                                if kt == CT - 1 and i == 2:
                                    mm.then_inc(y_done, 1)
                    if r < 3:
                        mm.then_inc(slot_used, 1)

            def tables(m):
                pe.wait_ge(oh_ready, m + 1)
                for i in range(TT * TOPK):
                    mm = nc.tensor.matmul(bank[4][0:CAP, 0:2 * NE], oha[:, i // TOPK, i % TOPK, :],
                                          ohb[:, i // TOPK, i % TOPK].rearrange("p w e -> p (w e)"),
                                          start=(i == 0), stop=(i == TT * TOPK - 1))
                mm.then_inc(tab_done, 1)

            def pass_end(passes):
                pe.wait_ge(xT_ready, passes * 2 * (NE + 1))
                pe.wait_ge(yr_ready, passes * 2 * NE + 2)

            tables(0)
            embed(range(5, 2 * TT))
            turn_x(0)
            pe.wait_ge(pp_ready, 2 * TT)
            with pe.Fori(0, NE) as e:
                expert(e, e)
            pass_end(1)
            pe.wait_ge(maxc_ready, 1)
            fullest = pe.value_load(maxc[0:1, 0:1], min_val=0, max_val=T)
            with pe.If(fullest > CAP):
                with pe.Fori(1, PASSES) as m:
                    with pe.If(fullest > m * CAP):
                        tables(m)
                        turn_x(m * (NE + 1))
                        with pe.Fori(0, NE) as e:
                            expert(m * NE + e, m * (NE + 1) + e)
                        pass_end(m + 1)
            pe.sem_inc(experts_left, 1)

            pe.wait_ge(wexp_ready, 1)
            for tt in range(TT):
                tr = nc.tensor.transpose(bank[6][0:NE, tt * P:(tt + 1) * P], wexp[:, tt, :], ident[:])
            tr.then_inc(wT_done, 1)
            pe.wait_ge(wT_ready, 1)
            pe.wait_ge(bdn_in, 16)
            for i in range(2 * TT):
                nc.tensor.matmul(bank[i][:], wexp_T[:, (i // 2) * P:(i // 2 + 1) * P],
                                 bdn[:, (i % 2) * NCOL:(i % 2 + 1) * NCOL], start=True, stop=True).then_inc(bias_done, 1)

            def turn_tile(tt):
                pe.wait_ge(x2_ready, tt + 1)
                if tt >= 2:
                    pe.wait_ge(x_lo_ready, 2 * tt - 2)
                for ct in range(CT):
                    tr = nc.tensor.transpose(bank[4 + 2 * (tt % 2) + ct // 4][:, (ct % 4) * P:(ct % 4 + 1) * P],
                                             x[:, tt, ct * P:(ct + 1) * P], ident[:])
                    if ct % 4 == 3:
                        tr.then_inc(x_turned, 1)

            def gate_product(tt, n2):
                if tt >= 2:
                    pe.wait_ge(gate_ready, 2 * (tt - 2) + n2 + 1)
                cols = slice(n2 * NCOL, (n2 + 1) * NCOL)
                for kt in range(CT):
                    s, kk = kt // 2, kt % 2
                    if tt == 0:
                        pe.wait_ge(pg_lo_ready, kt + 1)
                    if kt % 4 == 0:
                        pe.wait_ge(x_lo_ready, 2 * tt + kt // 4 + 1)
                    for i, (a, w) in enumerate(((x_hi, pg_hi), (x_hi, pg_lo), (x_lo, pg_hi))):
                        mm = nc.tensor.matmul(bank[2 * (tt % 2) + n2][:], a[:, tt, kt, :], w[s][:, kk, cols],
                                              start=(kt == 0 and i == 0), stop=(kt == CT - 1 and i == 2))
                mm.then_inc(pg_done, 1)

            turn_tile(0)
            turns = {(0, 0): (1,), (1, 0): (2,), (1, 1): (3,)}
            for tt in range(TT):
                for n2 in range(2):
                    gate_product(tt, n2)
                    for tile in turns.get((tt, n2), ()):
                        turn_tile(tile)

        @block.scalar
        def _(act):
            par_rows = [(t.g_mix, PR_MIX), (t.ret_gn_w, PR_GN), (t.b_dw, PR_BDW), (t.conv_ln_w, PR_LNW),
                        (t.conv_ln_b, PR_LNB), (t.b_conv_out, PR_BCO), (t.g_ffn, PR_FFN), (t.g_ple, PR_PLE)]
            for vec, first in par_rows:
                act.dma_start(rows[first:first + CT, 0, :], vec.rearrange("(c p) -> c p", p=P)).then_inc(par_in, 16)
            taps = t.w_dw.rearrange("k (c p) -> (k c) p", p=P)
            for i in range(2):
                act.dma_start(rows[0:TAP_ROWS, 1 + i, :], taps[i * TAP_ROWS:(i + 1) * TAP_ROWS]).then_inc(par_in, 16)
            act.dma_start(ident[:], t.ident).then_inc(par_in, 16)

            sq_chain = Chain(act, sq_own)

            def root_mean_squares(first, wait, out):
                for tt in range(TT):
                    wait(tt)
                    last = sq_chain.mark(nc.scalar.activation(out(tt), x[:, tt, :], ACT.Square,
                                                              accum_out=ss[:, first + tt:first + tt + 1]))
                act.wait_ge(eps_ready, 1)
                sq_chain.wait(last)
                group = ss[:, first:first + TT]
                nc.scalar.activation(group, group, ACT.Sqrt, bias=eps, scale=1.0 / D).then_inc(rms_ready, 1)

            root_mean_squares(0, lambda tt: act.wait_ge(x_in[tt], 16), lambda tt: xn[:, tt, :])

            def hi_part(c, s):
                act.wait_ge(raw_in[s], 16 * (c + 1))
                if c:
                    if s < 3:
                        act.wait_ge(gran_used, 3 * (c - 1) + s + 1)
                    else:
                        act.wait_ge(bank_done, 4 * c)
                nc.scalar.copy(whi[s][:], raw[s][:]).then_inc(hi_ready, 1)

            def turned_hi_part(i, hi, first, ct):
                act.wait_ge(turned, i + 1)
                nc.scalar.activation(hi[:, ct, :], bank[4 + i % 4][:], ACT.Copy,
                                     scale=col(first, ct)).then_inc(turned_hi, 1)

            def sigmoid_tile(c, b, out, done=bank_free):
                act.wait_ge(bank_done, 4 * c + b + 1)
                nc.scalar.activation(out, bank[b][:], ACT.Sigmoid).then_inc(done, 1)

            def k_turned(j):
                act.wait_ge(qkT_done, j + 1)
                nc.scalar.copy(k_T[:], bank[5][:].rearrange("p (h c) -> p h c", h=HEADS)).then_inc(kT_ready, 1)

            def evac(c):
                if c in (0, 2):
                    if c == 2:
                        act.wait_ge(bank_free, 8)
                    for b in range(4):
                        sigmoid_tile(c, b, sgb[:, b, :])
                elif c in (4, 5):
                    for b in range(4):
                        act.wait_ge(bank_done, 4 * c + b + 1)
                        nc.scalar.copy((q, k)[c - 4][:, b].rearrange("p h a r -> p (h a r)"),
                                       bank[b][:]).then_inc(bank_free, 1)
                elif c in (6, 7):
                    for b in range(4):
                        act.wait_ge(bank_done, 4 * c + b + 1)
                        nc.scalar.copy(v[:, b, (c - 6) * NCOL:(c - 5) * NCOL], bank[b][:]).then_inc(bank_free, 1)
                elif c in (8, 9):
                    for b in range(4):
                        if 4 * (c - 8) + b >= 2:
                            act.wait_ge(bank_free, 4 * c + b - 1)
                        sigmoid_tile(c, b, gs[b % 2][:], gs_ready)
                elif c in (10, 11):
                    if c == 10:
                        act.wait_ge(cv_ready, len(DVE_PAIRS))
                        act.wait_ge(cv_pool_ready, 1)
                    for b in range(4):
                        sigmoid_tile(c, b, sm_c[:, 4 * (c - 10) + b, :])
                elif c in (12, 13):
                    if c == 12:
                        act.wait_ge(out_used, TT)
                    for b in range(4):
                        sigmoid_tile(c, b, sm_r[:, 4 * (c - 12) + b, :])
                elif c in (16, 17):
                    for b in range(4):
                        i = 4 * (c - 16) + b
                        act.wait_ge(mix_ready, i + 1)
                        nc.scalar.copy(mx_hi[:, i, :], sm_c[:, i, :]).then_inc(mix_hi, 1)

            hi_part(0, 0)
            act.wait_ge(par_ready, 1)
            for ct in range(CT):
                turned_hi_part(ct, h_hi, PR_MIX, ct)
            for s in range(1, 4):
                hi_part(0, s)

            for c in range(1, CHUNKS):
                for s in range(4):
                    if s == 3:
                        evac(c - 1)
                        if c == 11:
                            k_turned(1)
                    hi_part(c, s)
                    if (c, s) in K_TURNED:
                        k_turned(K_TURNED[c, s])
                    for ct in RET_TURNED.get((c, s), ()):
                        turned_hi_part(CT + ct, r_hi, PR_GN, ct)
                if c == 13:
                    act.wait_ge(out_used, TT)
                    nc.scalar.activation(mv[:, :, :, 1], mv[:, :, :, 1], ACT.Sqrt, bias=eps).then_inc(dev_ready, 1)
                if c == 14:
                    for ct in range(CT):
                        act.wait_ge(ln_cent, ct + 1)
                        if ct >= 2:
                            act.wait_ge(ln_sq_used, ct - 1)
                        nc.scalar.square(sq[ct % 2][:], cv[:, ct, :]).then_inc(ln_sq, 1)
                if c == 15:
                    act.wait_ge(ln_sq_used, CT)
                    nc.scalar.activation(lrs[:], bank[5][:], ACT.Sqrt, bias=eps, scale=1.0 / D).then_inc(ln_dev, 1)
                    for ct in range(CT + 1):
                        if ct < CT:
                            act.wait_ge(ln_z, ct + 1)
                            if ct >= 2:
                                act.wait_ge(ln_val, ct - 1)
                            nc.scalar.activation(lsg[ct % 2][:], cv[:, ct, :], ACT.Sigmoid).then_inc(ln_sig, 1)
                        if ct:
                            act.wait_ge(ln_val, ct)
                            nc.scalar.copy(c_hi[:, ct - 1, :], cv[:, ct - 1, :]).then_inc(ln_hi, 1)
            for ct in range(CT):
                i = 2 * CT + ct
                act.wait_ge(turned, i + 1)
                nc.scalar.activation(f_T[:, ct, :], bank[4 + i % 4][:], ACT.Copy,
                                     scale=col(PR_FFN, ct)).then_inc(turned_out, 1)
            root_mean_squares(0, lambda tt: act.wait_ge(bank_free, 4 * (CHUNKS - 1) + tt + 1), lambda tt: xn2[:, tt, :])

            def embedded(tiles):
                for i in tiles:
                    act.wait_ge(pp_done, i + 1)
                    nc.scalar.copy(pp[:, i // 2, (i % 2) * NCOL:(i % 2 + 1) * NCOL],
                                   bank[2 + i % 2][:]).then_inc(pp_ready, 1)

            embedded(range(0, 3))
            act.wait_ge(lg_ready, 1)
            for tt in range(TT):
                nc.scalar.activation(wtop[:, tt, :], top[:, tt, 0:TOPK], ACT.Exp,
                                     bias=nmax[:, tt:tt + 1]).then_inc(exp_ready, 1)

            embedded(range(3, 2 * TT))
            act.wait_ge(hf_out, 16 * TT)

            def expert(n):
                for r in range(4):
                    act.wait_ge(w_in_s[GU_SLOTS + r], 16 * (n + 1))
                    nc.scalar.copy(dn_hi[r][:], wslot[GU_SLOTS + r][:]).then_inc(dn_hi_ready, 1)
                for i in range(5):
                    if i < 4:
                        act.wait_ge(z_ready, 4 * n + i + 1)
                        nc.scalar.activation(sg[i % 2][:], z[i % 2][:, 0], ACT.Sigmoid,
                                             scale=ALPHA).then_inc(sg_ready, 1)
                    if i >= 1:
                        act.wait_ge(act_ready, 4 * n + i + 2)
                        pair = slice(2 * i - 2, 2 * i)
                        nc.scalar.copy(act_hi[:, pair, :], act_T[:, pair, :]).then_inc(act_hi_ready, 1)
                act.wait_ge(rows_left, n + 1)
                for j in range(2):
                    act.wait_ge(y_done, 2 * n + j + 1)
                    nc.scalar.copy(yr[0:CAP, j * NCOL:(j + 1) * NCOL], bank[4 + j][0:CAP, :]).then_inc(yr_ready, 1)

            with act.Fori(0, NE) as e:
                expert(e)
            act.wait_ge(maxc_ready, 1)
            fullest = act.value_load(maxc[0:1, 0:1], min_val=0, max_val=T)
            with act.If(fullest > CAP):
                with act.Fori(1, PASSES) as m:
                    with act.If(fullest > m * CAP):
                        with act.Fori(0, NE) as e:
                            expert(m * NE + e)

            for kt in range(CT):
                s, kk = kt // 2, kt % 2
                if kk == 0:
                    act.wait_ge(raw_in[s], 16 * (CHUNKS + 1))
                nc.scalar.activation(pg_hi[s][:, kk, :], pg_raw[s][:, kk, :], ACT.Copy,
                                     scale=col(PR_PLE, kt)).then_inc(pg_hi_ready, 1)

            def square(tt, first):
                sq_chain.link(nc.scalar.activation(sq_out[:], x[:, tt, :], ACT.Square,
                                                   accum_out=ss[:, first + tt:first + tt + 1]))

            def rms(first, last):
                nc.scalar.activation(ss[:, first:last], ss[:, first:last], ACT.Sqrt, bias=eps,
                                     scale=1.0 / D).then_inc(rms_ready, 1)

            for tt in range(TT):
                for j in range(2):
                    act.wait_ge(x_turned, 2 * tt + j + 1)
                    nc.scalar.copy(x_hi[:, tt, 4 * j:4 * j + 4, :], bank[4 + 2 * (tt % 2) + j][:]
                                   .rearrange("p (c t) -> p c t", t=P)).then_inc(x_hi_ready, 1)
                square(tt, 0)
            rms(0, TT)
            act.wait_ge(inv_ready, 2)
            for tt in range(TT):
                for n2 in range(2):
                    i = 2 * tt + n2
                    if i >= 2:
                        act.wait_ge(x3_ready, i - 1)
                    act.wait_ge(pg_done, i + 1)
                    nc.scalar.activation(gate[n2][:], bank[2 * (tt % 2) + n2][:], ACT.Sigmoid,
                                         scale=ss[:, tt:tt + 1]).then_inc(gate_ready, 1)
                if tt:
                    act.wait_ge(x3_ready, 2 * tt)
                    square(tt - 1, TT)
                if tt == TT - 2:
                    rms(TT, 2 * TT - 2)
            act.wait_ge(x3_ready, 2 * TT)
            square(TT - 1, TT)
            rms(2 * TT - 2, 2 * TT)

        @block.gpsimd
        def _(pool):
            nc.gpsimd.memset(ones[:], 1.0).then_inc(pad_done, 1)
            nc.gpsimd.memset(cin[:, :, 0:TAPS - 1], 0.0).then_inc(pad_done, 1)
            nc.gpsimd.memset(tok_tab[:, NE:NE + 1], EMPTY).then_inc(pad_done, 1)
            nc.gpsimd.memset(eps, EPS).then_inc(eps_ready, 1)
            pool.dma_start(brow[:], t.b_gu).then_inc(tab_in, 16)
            pool.dma_start(cst[:, 0:164], t.cst[:, 0:164]).then_inc(tab_in, 16)
            pool.dma_start(tri[:], t.tri).then_inc(tab_in, 16)
            pool.dma_start(rope[:], t.rope.rearrange("p (a t h) -> p a t h", a=4, t=TT)).then_inc(tab_in, 16)
            pool.dma_start(dmask[:], t.dmask.rearrange("p (h c) -> p h c", h=HEADS)).then_inc(tab_in, 16)
            pool.dma_start(dq[:], t.dq.rearrange("p (h c) -> p h c", h=HEADS)).then_inc(tab_in, 16)
            pool.dma_start(w_rout[:], t.w_router.rearrange("(c p) e -> p c e", p=P)).then_inc(tab_in, 16)
            pool.dma_start(b_rout[:], t.b_router.partition_broadcast(P)).then_inc(tab_in, 16)

            own = Chain(pool, pool_own)

            def conv_taps(pair, taps, product):
                for kk in taps:
                    for ct in (2 * pair, 2 * pair + 1):
                        if kk == 0:
                            ins = nc.gpsimd.tensor_scalar(cv[:, ct, :], cin[:, ct, 0:T], tap(0, ct),
                                                          col(PR_BDW, ct), ALU.mult, ALU.add)
                        else:
                            own.link(nc.gpsimd.tensor_scalar(product[:], cin[:, ct, kk:kk + T], tap(kk, ct), None,
                                                             ALU.mult))
                            ins = nc.gpsimd.tensor_tensor(cv[:, ct, :], cv[:, ct, :], product[:], ALU.add)
                        if kk == TAPS - 1 and ct % 2:
                            ins.then_inc(cv_pool_ready, 1)
                        else:
                            own.link(ins)

            pool.wait_ge(bank_free, 8)
            pool.wait_ge(pad_done, 2)
            conv_taps(POOL_PAIR, range(0, TAPS // 2), tapped[0])
            for b in range(TT):
                pool.wait_ge(bank_free, 4 * (CH_QK + 1) + b + 1)
                rotate(nc.gpsimd, own, k, 2, b, rot_pa, rot_pb, k_ready, pool)
            pool.wait_ge(k_ready, TT)
            conv_taps(POOL_PAIR, range(TAPS // 2, TAPS), tapped[1])
            pool.wait_ge(cv_ready, len(DVE_PAIRS))
            pool.wait_ge(cv_pool_ready, 1)
            pool.wait_ge(out_used, TT)
            own.link(nc.gpsimd.tensor_tensor(lsum[:], cv[:, 0, :], cv[:, 1, :], ALU.add))
            for ct in range(2, CT - 1):
                own.link(nc.gpsimd.tensor_tensor(lsum[:], lsum[:], cv[:, ct, :], ALU.add))
            nc.gpsimd.tensor_tensor(lsum[:], lsum[:], cv[:, CT - 1, :], ALU.add).then_inc(ls_ready, 1)

            hf_t = hf_rows.rearrange("(t p) d -> t p d", p=P)
            pool.wait_ge(inv_ready, 1)
            for tt in range(TT):
                nc.gpsimd.tensor_scalar(xn2[:, tt, :], x[:, tt, :], ss[:, tt:tt + 1], None,
                                        ALU.mult).then_inc(xn2_own, 1)
                pool.wait_ge(xn2_own, tt + 1)
                pool.dma_start(hf_t[tt], xn2[:, tt, :]).then_inc(hf_out, 16)
            pool.wait_ge(rank_done, 1)
            nc.gpsimd.memset(xg[:], 0.0).then_inc(xg_zero, 1)
            pool.wait_ge(xg_zero, 1)
            pool.wait_ge(hf_out, 16 * TT)

            def wait_reg(sem, value):
                pool.wait_ge(sem, value)
                pool.sem_inc(pool_waited, 1)

            def gather(c, e):
                wait_reg(xt_done, 2 * c + 2)
                nc.gpsimd.tensor_copy(idx_g[0:CAP, :], tok_tab[0:CAP, bass.ds(e, 1)]).then_inc(idx_g_done, 1)
                wait_reg(idx_g_done, c + 1)
                nc.gpsimd.indirect_dma_start(
                    xg[0:CAP, :], None, hf_rows, bass.IndirectOffsetOnAxis(ap=idx_g[0:CAP, 0:1], axis=0),
                    bounds_check=T - 1, oob_is_err=False).then_inc(gathered, 16)

            def scatter(n, e):
                nc.gpsimd.tensor_copy(idx_s[0:CAP, :], asg_tab[0:CAP, bass.ds(e, 1)]).then_inc(idx_s_done, 1)
                wait_reg(idx_s_done, n + 1)
                wait_reg(yr_ready, 2 * n + 4)
                nc.gpsimd.indirect_dma_start(
                    y_rows, bass.IndirectOffsetOnAxis(ap=idx_s[0:CAP, 0:1], axis=0), yr[0:CAP, :], None,
                    bounds_check=T * TOPK - 1, oob_is_err=False).then_inc(scattered, 16)
                wait_reg(scattered, 16 * n + 16)
                pool.sem_inc(rows_left, 1)

            def one_pass(m):
                wait_reg(tab_ready, m + 1)
                gather(m * (NE + 1), 0)
                with pool.Fori(0, NE) as e:
                    gather(m * (NE + 1) + e + 1, e + 1)
                    scatter(m * NE + e, e)
                pool.sem_inc(pass_done, 1)

            one_pass(0)
            pool.wait_ge(maxc_ready, 1)
            fullest = pool.value_load(maxc[0:1, 0:1], min_val=0, max_val=T)
            with pool.If(fullest > CAP):
                with pool.Fori(1, PASSES) as m:
                    with pool.If(fullest > m * CAP):
                        one_pass(m)
            pool.sem_inc(moe_done, 1)

        @block.vector
        def _(dve):
            dve.sem_inc(act_ready, 2)
            dve.sem_inc(yr_ready, 2)
            dve.sem_inc(rows_left, 1)
            dve.sem_inc(xt_done, 2)
            own = Chain(dve, dve_own)
            V = nc.vector

            def inverse_rms(group, first, last):
                dve.wait_ge(rms_ready, group + 1)
                ins = V.reciprocal(ss[:, first:last], ss[:, first:last])
                own.mark(ins)
                own.wait(own.n)

            def lo_part(c, s):
                dve.wait_ge(hi_ready, 4 * c + s + 1)
                V.tensor_tensor(wlo[s][:], raw[s][:], whi[s][:].bitcast(F32), ALU.subtract).then_inc(lo_ready, 1)

            def turned_lo_part(i, hi_count, hi, lo, first, ct):
                dve.wait_ge(turned_hi, hi_count)
                V.scalar_tensor_tensor(lo[:, ct, :], bank[4 + i % 4][:], col(first, ct), hi[:, ct, :].bitcast(F32),
                                       ALU.mult, ALU.subtract).then_inc(turned_out, 1)

            inverse_rms(0, 0, TT)
            for tt in range(TT):
                V.tensor_scalar(xn[:, tt, :], x[:, tt, :], ss[:, tt:tt + 1], None, ALU.mult).then_inc(xn_ready, 1)
            dve.wait_ge(par_done, 1)
            V.tensor_copy(par[:], bank[4][:, 0:64])
            V.tensor_copy(wdw[:].rearrange("p a r -> p (a r)"),
                          bank[4][:, 64:64 + 2 * TAP_ROWS]).then_inc(par_ready, 1)
            dve.wait_ge(par_ready, 1)
            lo_part(0, 0)
            for ct in range(CT):
                turned_lo_part(ct, ct + 1, h_hi, h_lo, PR_MIX, ct)
            for s in range(1, 4):
                lo_part(0, s)

            last_tap = {}
            conv_steps = [(pair, kk, ct) for pair in DVE_PAIRS for kk in range(TAPS) for ct in (2 * pair, 2 * pair + 1)]
            assert 4 * sum(CONV_STEPS.values()) + CONV_START >= len(conv_steps)

            def conv(steps):
                for pair, kk, ct in steps:
                    if kk == 0 and ct % 2 == 0:
                        dve.wait_ge(bank_free, 8 if pair < 2 else 16)
                        dve.wait_ge(pad_done, 2)
                    if kk == 0:
                        ins = V.tensor_scalar(cv[:, ct, :], cin[:, ct, 0:T], tap(0, ct), col(PR_BDW, ct),
                                              ALU.mult, ALU.add)
                    else:
                        own.wait(last_tap[ct])
                        ins = V.scalar_tensor_tensor(cv[:, ct, :], cin[:, ct, kk:kk + T], tap(kk, ct),
                                                     cv[:, ct, :], ALU.mult, ALU.add)
                    if kk == TAPS - 1 and ct % 2:
                        ins.then_inc(cv_ready, 1)
                    else:
                        last_tap[ct] = own.mark(ins)

            def evac(c):
                for b in range(4):
                    def done():
                        dve.wait_ge(bank_done, 4 * c + b + 1)
                    if c in (1, 3):
                        done()
                        V.tensor_tensor(cin[:, 2 * (c - 1) + b, TAPS - 1:], bank[b][:], sgb[:, b, :],
                                        ALU.mult).then_inc(bank_free, 1)
                    elif c in (8, 9):
                        dve.wait_ge(gs_ready, 4 * (c - 8) + b + 1)
                        V.tensor_tensor(g[:, b, (c - 8) * NCOL:(c - 7) * NCOL], bank[b][:], gs[b % 2][:],
                                        ALU.mult).then_inc(bank_free, 1)
                    elif c in (14, 15):
                        i = 4 * (c - 14) + b
                        done()
                        V.tensor_tensor(sm_r[:, i, :], bank[b][:], sm_r[:, i, :], ALU.mult).then_inc(bank_free, 1)
                    elif c in (16, 17):
                        i = 4 * (c - 16) + b
                        done()
                        V.scalar_tensor_tensor(sm_c[:, i, :], bank[b][:], col(PR_BCO, i), sm_c[:, i, :],
                                               ALU.add, ALU.mult).then_inc(bank_free, 1)
                    elif c in (18, 19):
                        done()
                        xs = x[:, b, (c - 18) * NCOL:(c - 17) * NCOL]
                        V.tensor_tensor(xs, bank[b][:], xs, ALU.add).then_inc(bank_free, 1)
                if c in (16, 17):
                    tiles = range(4 * (c - 16), 4 * (c - 16) + 4)
                    for i in tiles:
                        dve.wait_ge(bank_free, 4 * 16 + i + 1)
                        V.tensor_tensor(sm_c[:, i, :], sm_c[:, i, :], sm_r[:, i, :], ALU.add).then_inc(mix_ready, 1)
                    for i in tiles:
                        dve.wait_ge(mix_hi, i + 1)
                        V.tensor_tensor(mx_lo[:, i, :], sm_c[:, i, :], mx_hi[:, i, :].bitcast(F32),
                                        ALU.subtract).then_inc(mix_lo, 1)

            def turned_qk(j):
                dve.wait_ge(qkT_done, j + 1)
                src = bank[4][:].rearrange("p (h c) -> p h c", h=HEADS)
                V.tensor_copy(q_T[:], src)
                V.tensor_tensor(qd_T[:], src, dq[:], ALU.mult)
                V.tensor_tensor(kd[:], k[:, j].rearrange("p h a r -> p h (a r)"),
                                dk_col.unsqueeze(2).to_broadcast([P, HEADS, DK]), ALU.mult).then_inc(qT_ready, 1)

            def decay_scores(j):
                dve.wait_ge(sc_done, j + 1)
                V.tensor_tensor(s_T[:], bank[6][:].rearrange("p (h c) -> p h c", h=HEADS), dmask[:],
                                ALU.mult).then_inc(sT_ready, 1)

            def gate_outputs(j):
                dve.wait_ge(out_done, j + 1)
                o = [bank[4 + h // 2][:, (h % 2) * DV:(h % 2 + 1) * DV] for h in range(HEADS)]
                for h in range(HEADS):
                    m1 = own.mark(V.bn_stats(bn[:, h, :], o[h]))
                own.wait(m1)
                for h in range(HEADS):
                    m1 = own.mark(V.bn_aggr(mv[:, j, h, :], bn[:, h, :]))
                own.wait(m1)
                for h in range(HEADS):
                    gh = g[:, j, h * DV:(h + 1) * DV]
                    ins = V.scalar_tensor_tensor(gh, o[h], mv[:, j, h, 0:1], gh, ALU.subtract, ALU.mult)
                ins.then_inc(out_used, 1)
                if j < TT - 1:
                    dve.wait_ge(st_done, j + 1)
                    for h in range(HEADS):
                        inc = bank[6 + h // 2][:, (h % 2) * DV:(h % 2 + 1) * DV]
                        if j == 0:
                            ins = V.tensor_copy(state[:, h, :], inc)
                        else:
                            ins = V.scalar_tensor_tensor(state[:, h, :], state[:, h, :], CHUNK_DECAY[h], inc,
                                                         ALU.mult, ALU.add)
                    ins.then_inc(state_ready, 1)

            behind = {(10, 3): ((turned_qk, 0), (decay_scores, 0), (gate_outputs, 0)),
                      (11, 0): ((turned_qk, 1),), (11, 1): ((decay_scores, 1),), (11, 2): ((gate_outputs, 1),),
                      (11, 3): ((turned_qk, 2), (decay_scores, 2)),
                      (12, 0): ((gate_outputs, 2),), (12, 1): ((turned_qk, 3),), (12, 2): ((decay_scores, 3),),
                      (12, 3): ((gate_outputs, 3),)}

            for c in range(1, CHUNKS):
                for s in range(4):
                    if s == 3:
                        evac(c - 1)
                    lo_part(c, s)
                    if c == 1 and s == 0:
                        dve.wait_ge(bexp_done, 1)
                        V.tensor_copy(bexp[:], bank[4][:].rearrange("p (m e) -> p e m", e=NE)).then_inc(bexp_ready, 1)
                    if c == 6:
                        rotate(V, own, q, 0, s, rot_a, rot_b, q_ready, dve)
                    steps = CONV_START if (c, s) == (2, 3) else CONV_STEPS.get(c, 0)
                    conv(conv_steps[:steps])
                    conv_steps = conv_steps[steps:]
                    for f, j in behind.get((c, s), ()):
                        f(j)
                    for ct in RET_TURNED.get((c, s), ()):
                        turned_lo_part(CT + ct, CT + ct + 1, r_hi, r_lo, PR_GN, ct)
                if c == 13:
                    dve.wait_ge(dev_ready, 1)
                    own.link(V.reciprocal(mv[:, :, :, 1], mv[:, :, :, 1]))
                    for j in range(TT):
                        for h in range(HEADS):
                            gh = g[:, j, h * DV:(h + 1) * DV]
                            ins = V.tensor_scalar(gh, gh, mv[:, j, h, 1:2], None, ALU.mult)
                    ins.then_inc(gated, 1)
                if c == 14:
                    dve.wait_ge(ln_mean, 1)
                    for ct in range(CT):
                        V.scalar_tensor_tensor(cv[:, ct, :], bank[4][:], -1.0 / D, cv[:, ct, :],
                                               ALU.mult, ALU.add).then_inc(ln_cent, 1)
                if c == 15:
                    dve.wait_ge(ln_dev, 1)
                    own.link(V.reciprocal(lrs[:], lrs[:]))
                    for i in range(CT + 2):
                        if i < CT:
                            own.link(V.tensor_tensor(cv[:, i, :], cv[:, i, :], lrs[:], ALU.mult))
                            V.tensor_scalar(cv[:, i, :], cv[:, i, :], col(PR_LNW, i), col(PR_LNB, i),
                                            ALU.mult, ALU.add).then_inc(ln_z, 1)
                        if 1 <= i <= CT:
                            dve.wait_ge(ln_sig, i)
                            V.tensor_tensor(cv[:, i - 1, :], cv[:, i - 1, :], lsg[(i - 1) % 2][:],
                                            ALU.mult).then_inc(ln_val, 1)
                        if i >= 2:
                            dve.wait_ge(ln_hi, i - 1)
                            V.tensor_tensor(c_lo[:, i - 2, :], cv[:, i - 2, :], c_hi[:, i - 2, :].bitcast(F32),
                                            ALU.subtract).then_inc(c_ready, 1)
            evac(CHUNKS - 1)
            dve.wait_ge(pT_done, 1)
            for kt in range(2):
                ins = V.tensor_copy(p_T[:, kt, :], bank[2 + kt][:])
            ins.then_inc(pT_ready, 1)

            inverse_rms(1, 0, TT)
            dve.sem_inc(inv_ready, 1)
            dve.wait_ge(lg_done, 1)
            for tt in range(TT):
                ins = V.scalar_tensor_tensor(lg[:, tt, :], bank[0][:, tt * NE:(tt + 1) * NE], ss[:, tt:tt + 1],
                                             b_rout[:], ALU.mult, ALU.add)
            own.link(ins)
            marks = [own.mark(V.max(top[:, tt, :], lg[:, tt, :])) for tt in range(TT)]
            for tt in range(TT):
                own.wait(marks[tt])
                ins = V.max_index(topi[:, tt, :], top[:, tt, :], lg[:, tt, :])
            own.link(ins)
            V.tensor_scalar(nmax, top[:, :, 0], -1.0, None, ALU.mult).then_inc(lg_ready, 1)
            own.link(V.tensor_copy(topf[:], topi[:, :, 0:TOPK]))
            hot = [P, TT, TOPK, NE]
            own.link(V.tensor_tensor(oh[:], iota_e.unsqueeze(1).unsqueeze(1).to_broadcast(hot),
                                     topf[:].unsqueeze(3).to_broadcast(hot), ALU.is_equal))
            V.tensor_reduce(msk[:], oh[:].rearrange("p t k e -> p t e k"), AX_X, ALU.add).then_inc(msk_ready, 1)
            for w in range(2):
                V.tensor_tensor(ohb[:, :, :, w, :], oh[:], ids[:, w].unsqueeze(3).to_broadcast(hot), ALU.mult)
            dve.wait_ge(rank_done, 1)
            V.tensor_reduce(maxc[:], bank[1][0:1, TT * NE:(TT + 1) * NE], AX_X, ALU.max).then_inc(maxc_ready, 1)
            own.link(V.tensor_tensor(prod[:], oh[:], bank[1][:, 0:TT * NE].rearrange("p (t e) -> p t e", e=NE)
                                     .unsqueeze(2).to_broadcast(hot), ALU.mult))
            own.link(V.tensor_reduce(rank, prod[:], AX_X, ALU.add))

            def slot_tables(m, chain):
                caps = [P, TT * TOPK, CAP]
                V.tensor_tensor(oha[:].rearrange("p t k c -> p (t k) c"), iota_cap.unsqueeze(1).to_broadcast(caps),
                                rank.rearrange("p t k -> p (t k)").unsqueeze(2).to_broadcast(caps),
                                ALU.is_equal).then_inc(oh_ready, 1)
                dve.wait_ge(oh_ready, m + 1)
                chain.link(V.tensor_scalar(rank, rank, -float(CAP), None, ALU.add))
                dve.wait_ge(tab_done, m + 1)
                V.tensor_scalar(tok_tab[0:CAP, 0:NE], bank[4][0:CAP, NE:2 * NE], float(EMPTY), None, ALU.add)
                V.tensor_scalar(asg_tab[0:CAP, 0:NE], bank[4][0:CAP, 0:NE], float(EMPTY), None,
                                ALU.add).then_inc(tab_ready, 1)

            slot_tables(0, own)
            dve.wait_ge(exp_ready, TT)
            own.link(V.tensor_reduce(wsum, wtop, AX_X, ALU.add))
            own.link(V.reciprocal(wsum, wsum))
            own.link(V.tensor_tensor(wtop, wtop, wsum.unsqueeze(2).to_broadcast([P, TT, TOPK]), ALU.mult))

            def turned_x(c, j):
                dve.wait_ge(xt_done, 2 * c + j + 3)
                V.tensor_tensor(x_T[:, 4 * j:4 * j + 4, :], bank[6 + j][:, 0:4 * CAP].rearrange("p (k c) -> p k c", c=CAP),
                                par[:, PR_FFN + 4 * j:PR_FFN + 4 * j + 4].unsqueeze(2).to_broadcast([P, 4, CAP]),
                                ALU.mult).then_inc(xT_ready, 1)

            LINKS = 12

            def split_down(n, r):
                dve.wait_ge(dn_hi_ready, 4 * n + r + 1)
                V.tensor_tensor(dn_lo[r][:], wslot[GU_SLOTS + r][:], dn_hi[r][:].bitcast(F32),
                                ALU.subtract).then_inc(dn_lo_ready, 1)

            def expert(n, c, e):
                chain = Chain(dve, dve_moe, n * LINKS)
                bias = bexp[:, bass.ds(e, 1), :]
                for r in range(4):
                    split_down(n, r)
                for i in range(5):
                    if i < 4:
                        zb = z[i % 2]
                        dve.wait_ge(act_ready, 4 * n + i + 1)
                        dve.wait_ge(gu_done, 4 * n + i + 1)
                        for half in range(2):
                            bb = bias[:, :, CT * half + 2 * i:CT * half + 2 * i + 2].rearrange("p o i -> p (o i)")
                            ins = V.tensor_tensor(zb[:, half], bank[i][:, half * 2 * CAP:(half + 1) * 2 * CAP]
                                                  .rearrange("p (i c) -> p i c", c=CAP),
                                                  bb.unsqueeze(2).to_broadcast([P, 2, CAP]), ALU.add)
                        chain.link(ins)
                        V.tensor_scalar(zb[:], zb[:], LIMIT, None, ALU.min).then_inc(z_ready, 1)
                        dve.wait_ge(z_ready, 4 * n + i + 1)
                        chain.link(V.tensor_scalar(zb[:, 1], zb[:, 1], -LIMIT, 1.0, ALU.max, ALU.add))
                        chain.link(V.tensor_tensor(gu[i % 2][:], zb[:, 0], zb[:, 1], ALU.mult))
                    if i >= 1:
                        b = i - 1
                        dve.wait_ge(sg_ready, 4 * n + b + 1)
                        V.tensor_tensor(act_T[:, 2 * b:2 * b + 2, :], gu[b % 2][:], sg[b % 2][:],
                                        ALU.mult).then_inc(act_ready, 1)
                        dve.wait_ge(act_hi_ready, 4 * n + b + 1)
                        V.tensor_tensor(act_lo[:, 2 * b:2 * b + 2, :], act_T[:, 2 * b:2 * b + 2, :],
                                        act_hi[:, 2 * b:2 * b + 2, :].bitcast(F32), ALU.subtract) \
                            .then_inc(act_lo_ready, 1)
                assert chain.n == LINKS
                for j in range(2):
                    turned_x(c + 1, j)

            for j in range(2):
                turned_x(0, j)
            own.link(V.tensor_tensor(prod[:], oh[:], wtop.unsqueeze(3).to_broadcast(hot), ALU.mult))
            V.tensor_reduce(wexp[:], prod[:].rearrange("p t k e -> p t e k"), AX_X, ALU.add).then_inc(wexp_ready, 1)
            with dve.Fori(0, NE) as e:
                expert(e, e, e)
            dve.wait_ge(maxc_ready, 1)
            fullest = dve.value_load(maxc[0:1, 0:1], min_val=0, max_val=T)
            with dve.If(fullest > CAP):
                with dve.Fori(1, PASSES) as m:
                    with dve.If(fullest > m * CAP):
                        dve.wait_ge(pass_done, m)
                        slot_tables(m, Chain(dve, dve_pass, m - 1))
                        for j in range(2):
                            turned_x(m * (NE + 1), j)
                        with dve.Fori(0, NE) as e:
                            expert(m * NE + e, m * (NE + 1) + e, e)

            dve.wait_ge(wT_done, 1)
            V.tensor_copy(wexp_T[:], bank[6][0:NE, :]).then_inc(wT_ready, 1)

            def split_gate(kt):
                s, kk = kt // 2, kt % 2
                dve.wait_ge(pg_hi_ready, kt + 1)
                V.scalar_tensor_tensor(pg_lo[s][:, kk, :], pg_raw[s][:, kk, :], col(PR_PLE, kt),
                                       pg_hi[s][:, kk, :].bitcast(F32), ALU.mult, ALU.subtract).then_inc(pg_lo_ready, 1)

            def split_x(tt, j):
                dve.wait_ge(x_hi_ready, 2 * tt + j + 1)
                V.tensor_tensor(x_lo[:, tt, 4 * j:4 * j + 4, :], bank[4 + 2 * (tt % 2) + j][:]
                                .rearrange("p (c t) -> p c t", t=P), x_hi[:, tt, 4 * j:4 * j + 4, :].bitcast(F32),
                                ALU.subtract).then_inc(x_lo_ready, 1)

            def finish(group, first, last):
                inverse_rms(group, TT + first, TT + last)
                for tt in range(first, last):
                    V.scalar_tensor_tensor(x[:, tt, :], x[:, tt, :], ss[:, TT + tt:TT + tt + 1], g_fin[:],
                                           ALU.mult, ALU.mult).then_inc(fin_ready, 1)

            for kt in range(CT):
                split_gate(kt)
            for i in range(2 * TT):
                dve.wait_ge(bias_done, i + 1)
                xs = x[:, i // 2, (i % 2) * NCOL:(i % 2 + 1) * NCOL]
                added = own.mark(V.tensor_tensor(xs, bank[i][:], xs, ALU.add))
            own.wait(added)
            for tt in range(TT):
                dve.wait_ge(yb_in[tt], 16)
                for kk in range(TOPK):
                    ins = V.scalar_tensor_tensor(x[:, tt, :], yb[tt % 3][:, kk, :], wtop[:, tt, kk:kk + 1],
                                                 x[:, tt, :], ALU.mult, ALU.add)
                    if kk < TOPK - 1:
                        own.link(ins)
                    if tt and kk in (1, 2):
                        split_x(tt - 1, kk - 1)
                ins.then_inc(x2_ready, 1)
            for j in range(2):
                split_x(TT - 1, j)
            inverse_rms(2, 0, TT)
            dve.sem_inc(inv_ready, 1)
            for tt in range(TT):
                for n2 in range(2):
                    i = 2 * tt + n2
                    xs = x[:, tt, n2 * NCOL:(n2 + 1) * NCOL]
                    dve.wait_ge(gate_ready, i + 1)
                    V.tensor_tensor(gate[n2][:], gate[n2][:], pp[:, tt, n2 * NCOL:(n2 + 1) * NCOL],
                                    ALU.mult).then_inc(gate_used, 1)
                    dve.wait_ge(gate_used, i + 1)
                    V.tensor_tensor(xs, xs, gate[n2][:], ALU.add).then_inc(x3_ready, 1)
                if tt == TT - 2:
                    dve.wait_ge(g_fin_in, 16)
                    finish(3, 0, TT - 2)
            finish(4, TT - 2, TT)


def constants():
    import numpy as np
    f = np.float32
    token = np.arange(T, dtype=f)
    inv_freq = (f(10000.0) ** (-np.arange(HALF, dtype=f) / f(HALF))).astype(f)
    ang = (token[:, None] * inv_freq[None, :]).astype(f)
    cos, sin, scale = np.cos(ang), np.sin(ang), f(DK ** -0.5)
    rope = np.stack([cos, sin, cos * scale, sin * scale]).reshape(4, TT, P, HALF).transpose(2, 0, 1, 3)
    log_gamma = np.log1p(-np.exp2(-5.0 - np.arange(HEADS)))
    i = np.arange(P)
    rel = i[None, :] - i[:, None]
    dmask = np.where(rel[:, None, :] >= 0, np.exp(log_gamma[None, :, None] * np.maximum(rel, 0)[:, None, :]), 0.0)
    dq = np.broadcast_to(np.exp(log_gamma[:, None] * (i + 1.0))[None], (P, HEADS, P))
    cst = np.zeros((P, 168))
    cst[:, 0:CAP] = np.arange(CAP)
    cst[:, 96:128] = np.arange(NE)
    tok = np.arange(TT)[None, :, None] * P + i[:, None, None]
    cst[:, 128:144] = (tok * TOPK + np.arange(TOPK) - EMPTY).reshape(P, 16)
    cst[:, 144:160] = np.broadcast_to(tok - EMPTY, (P, TT, TOPK)).reshape(P, 16)
    cst[:, 164] = EPS
    cst[:, 160:164] = np.exp(log_gamma[None, :] * (P - 1.0 - i[:, None]))
    out = dict(ident=np.eye(P), tri=(i[:, None] < i[None, :]), cst=cst, rope=rope.reshape(P, -1),
               dmask=dmask.reshape(P, -1), dq=dq.reshape(P, -1))
    return {n: np.ascontiguousarray(a.astype(f)) for n, a in out.items()}


_INS = ["x", "p", "g_mix", "w_in", "ret_gn_w", "w_ret_out", "w_dw", "b_dw", "conv_ln_w", "conv_ln_b", "w_conv_out",
        "b_conv_out", "w_o", "g_ffn", "w_router", "b_router", "w_gu", "b_gu", "w_down", "b_down", "g_ple",
        "w_ple_gate", "w_ple_proj", "g_final"]


def kernel(**inputs):
    import types

    import numpy as np
    import concourse.bacc as bacc
    from concourse.bass_utils import run_bass_kernel_spmd

    nc = bacc.Bacc("TRN2", target_bir_lowering=False, num_devices=1)
    arrays, views = {}, {}
    for name in _INS:
        a = np.ascontiguousarray(inputs[name])
        if name == "x":
            a = a.reshape(T, D)
        elif name == "p":
            a = a.reshape(T, PLE)
        elif name != "g_final":
            a = a.reshape(a.shape[1:])
        arrays["in_" + name] = a
        views[name] = nc.dram_tensor("in_" + name, a.shape, F32, kind="ExternalInput").ap()
    for name, a in constants().items():
        arrays["const_" + name] = a
        views[name] = nc.dram_tensor("const_" + name, a.shape, F32, kind="ExternalInput").ap()
    views["out"] = nc.dram_tensor("out", (T, D), F32, kind="ExternalOutput").ap()
    build_layer(nc, types.SimpleNamespace(**views))
    r = run_bass_kernel_spmd(nc, [arrays], core_ids=[0])
    return r.results[0]["out"].reshape(1, T, D)
```

```python
from contextlib import ExitStack

import concourse.bass as bass
from concourse import mybir
from concourse.alu_op_type import AluOpType as ALU

F32 = mybir.dt.float32
F32R = mybir.dt.float32r
I32 = mybir.dt.int32
U32 = mybir.dt.uint32
ACT = mybir.ActivationFunctionType
AX_X = mybir.AxisListType.X

P = 128
T = 512
D = 1024
TT = T // P
CT = D // P
NCOL = 512
HEADS, DK, DV = 4, 128, 256
HALF = DK // 2
TAPS = 31
NE, TOPK = 32, 4
FF = 1024
PLE = 256
LIMIT, ALPHA = 7.0, 1.702
EPS = 1e-6
CAP = 96
PASSES = -(-T // CAP)
EMPTY = 4096
SLOTS = 12
GU_SLOTS = 8

COL_Q = 0
COL_GLU_A, COL_GLU_B, COL_MRET, COL_MCONV = 3 * D, 4 * D, 5 * D, 6 * D

CH_GLU, CH_QK, CH_V, CH_G, CH_MC, CH_MR, CH_YR, CH_YC, CH_WO, CHUNKS = 0, 4, 6, 8, 10, 12, 14, 16, 18, 20
CHUNK_DECAY = [(1.0 - 2.0 ** (-5 - h)) ** P for h in range(HEADS)]
DVE_PAIRS, POOL_PAIR = (0, 1, 2), 3
CONV_STEPS = {3: 6, 4: 5, 5: 6, 6: 4, 7: 6, 8: 5, 9: 5, 10: 5, 11: 3}
CONV_START = 6
TAP_STEPS = {5: (3,) * 4, 6: (3,) * 4, 8: (3,) * 4, 9: (4,) * 4, 10: (4, 4)}

TAP_ROWS = TAPS * CT // 2

PR_MIX, PR_GN, PR_BDW, PR_LNW, PR_LNB, PR_BCO, PR_FFN, PR_PLE = (8 * i for i in range(8))


class Chain:

    def __init__(self, eng, sem, base=0):
        self.eng, self.sem, self.base, self.n = eng, sem, base, 0

    def mark(self, ins):
        ins.then_inc(self.sem, 1)
        self.n += 1
        return self.n

    def wait(self, n):
        self.eng.wait_ge(self.sem, self.base + n)

    def link(self, ins):
        self.wait(self.mark(ins))


def build_layer(nc, t):
    with ExitStack() as ctx:
        base = -(-nc.sbuf_base // 64) * 64

        def at(name, kb, shape, dt=F32):
            return nc.alloc_sbuf_tensor_at(name, shape, dt, offset=base + int(kb * 1024))

        def sem(name):
            return ctx.enter_context(nc.semaphore(name))

        bank = [ctx.enter_context(nc.psum_tensor(f"bank{i}", [P, 512], F32)) for i in range(8)]

        x = at("x", 0, [P, TT, D])
        ident = at("ident", 16, [P, P])
        par = at("par", 16.5, [P, 64])
        wdw = at("wdw", 16.75, [P, 2, TAP_ROWS])
        bexp = at("bexp", 17.75, [P, NE, 16])
        w_rout = at("w_rout", 20.75, [P, CT, NE])
        b_rout = at("b_rout", 21.75, [P, NE])
        small = at("small", 21.875, [P, 48])
        ss = small[:, 0:8]
        rank = small[:, 8:24].rearrange("p (t k) -> p t k", k=TOPK)
        wtop = small[:, 24:40].rearrange("p (t k) -> p t k", k=TOPK)
        wsum = small[:, 40:44]
        nmax = small[:, 44:48]
        maxc = at("maxc", 22.0625, [1, 1], I32)
        ones = at("ones", 22.125, [P, P])
        tri = at("tri", 22.625, [P, P])
        cst = at("cst", 23.125, [P, 168])
        iota_cap, iota_e = cst[:, 0:CAP], cst[:, 96:128]
        ids = cst[:, 128:160].rearrange("p (w t k) -> p w t k", w=2, k=TOPK)
        dk_col, eps = cst[:, 160:164], cst[:, 164:165]
        tok_tab = at("tok_tab", 23.8125, [P, NE + 1], U32)
        asg_tab = at("asg_tab", 23.96875, [P, NE + 1], U32)
        idx_g = at("idx_g", 24.125, [P, 1], U32)
        idx_s = at("idx_s", 24.15625, [P, 1], U32)
        M = 24.1875
        raw = [at(f"raw{s}", M + 4 * s, [P, 2, NCOL]) for s in range(4)]
        whi = [at(f"whi{s}", M + 16 + 4 * s, [P, 2, NCOL], F32R) for s in range(4)]
        wlo = [at(f"wlo{s}", M + 32 + 4 * s, [P, 2, NCOL], F32R) for s in range(4)]
        h_hi = at("h_hi", M + 48, [P, CT, T], F32R)
        h_lo = at("h_lo", M + 64, [P, CT, T], F32R)
        cin = at("cin", M + 80, [P, CT, T + TAPS - 1])
        cv = at("cv", M + 97, [P, CT, T])
        q = at("q", M + 113, [P, TT, HEADS, 2, HALF])
        k = at("k", M + 121, [P, TT, HEADS, 2, HALF])
        v = at("v", M + 129, [P, TT, D])
        g = at("g", M + 145, [P, TT, D])
        xn = at("xn", M + 145, [P, TT, D])
        rows = at("rows", M + 113, [P, 3, P])
        brow = at("brow", M + 117, [NE, 2 * FF])
        R = M + 161
        rope = at("rope", R, [P, 4, TT, HALF])
        dmask = at("dmask", R + 20, [P, HEADS, P])
        dq = at("dq", R + 18, [P, HEADS, P])
        sgb = at("sgb", R + 4, [P, 4, T])
        gs = [at(f"gs{i}", R + 8 + 2 * i, [P, T]) for i in range(2)]
        rot_a = at("rot_a", R + 14, [P, HEADS, 2, HALF])
        rot_b = at("rot_b", R + 16, [P, HEADS, 2, HALF])
        rot_pa = at("rot_pa", R + 8, [P, HEADS, 2, HALF])
        rot_pb = at("rot_pb", R + 10, [P, HEADS, 2, HALF])
        tapped = [at(f"tapped{i}", R + kb, [P, T]) for i, kb in enumerate([4, 6, 12])]
        q_T = at("q_T", R + 8, [P, HEADS, P])
        qd_T = at("qd_T", R + 10, [P, HEADS, P])
        k_T = at("k_T", R + 6, [P, HEADS, P])
        s_T = at("s_T", R + 12, [P, HEADS, P])
        kd = at("kd", R + 4, [P, HEADS, DK])
        state = at("state", R + 14, [P, HEADS, DV])
        bn = at("bn", R + 22, [P, HEADS, 6])
        mv = small[:, 8:40].rearrange("p (t h a) -> p t h a", h=HEADS, a=2)
        sm_c = at("sm_c", M + 80, [P, CT, T])
        sm_r = at("sm_r", R, [P, CT, T])
        r_hi = at("r_hi", M + 113, [P, CT, T], F32R)
        r_lo = at("r_lo", M + 129, [P, CT, T], F32R)
        c_hi = at("c_hi", M + 145, [P, CT, T], F32R)
        c_lo = at("c_lo", M + 97, [P, CT, T], F32R)
        sq = [at(f"sq{i}", R + 16 + 2 * i, [P, T]) for i in range(2)]
        lsum = at("lsum", R + 20, [P, T])
        lrs = at("lrs", R + 20, [P, T])
        lsg = [at(f"lsg{i}", R + 16 + 2 * i, [P, T]) for i in range(2)]
        mx_hi = at("mx_hi", M + 113, [P, CT, T], F32R)
        mx_lo = at("mx_lo", M + 129, [P, CT, T], F32R)
        xn2 = at("xn2", M + 32, [P, TT, D])
        f_T = at("f_T", M + 113, [P, CT, T])
        p_in = at("p_in", M, [P, TT, PLE])
        wpp = at("wpp", M + 8, [P, 2, D])
        p_T = at("p_T", M + 129, [P, 2, T])
        lg_T = at("lg_T", M + 133, [NE, T])
        pp = at("pp", M + 16, [P, TT, D])
        lg = at("lg", R + 20, [P, TT, NE])
        msk = at("msk", R + 20.5, [P, TT, NE])
        top = at("top", R + 21, [P, TT, 8])
        topi = at("topi", R + 21.125, [P, TT, 8], U32)
        topf = at("topf", R + 21.25, [P, TT, TOPK])
        oh = at("oh", M + 142, [P, TT, TOPK, NE])
        prod = at("prod", M + 136, [P, TT, TOPK, NE])
        oha = at("oha", M + 136, [P, TT, TOPK, CAP])
        ohb = at("ohb", M + 161, [P, TT, TOPK, 2, NE])
        wslot = [at(f"wslot{s}", M + kb, [P, 2 * D]) for s, kb in
                 enumerate([48, 56, 64, 72, 80, 88, 97, 105, 145, 153, 165, 173])]
        xg = at("xg", M + 113, [P, D])
        x_T = at("x_T", M + 117, [P, CT, CAP])
        z = [at(f"z{i}", M + 120 + 1.5 * i, [P, 2, 2, CAP]) for i in range(2)]
        sg = [at(f"sg{i}", M + 123 + 0.75 * i, [P, 2, CAP]) for i in range(2)]
        gu = [at(f"gu{i}", M + 124.5 + 0.75 * i, [P, 2, CAP]) for i in range(2)]
        act_T = at("act_T", M + 126, [P, CT, CAP])
        act_lo = at("act_lo", M + 126, [P, CT, CAP], F32R)
        act_hi = at("act_hi", M + 129, [P, CT, CAP], F32R)
        dn_hi = [at(f"dn_hi{r}", M + kb, [P, 2 * D], F32R) for r, kb in enumerate([0, 8, 32, 40])]
        dn_lo = [at(f"dn_lo{r}", M + kb, [P, 2 * D], F32R) for r, kb in enumerate([145, 153, 165, 173])]
        wexp = at("wexp", M + 144, [P, TT, NE])
        yr = at("yr", M + 132, [P, D])
        yb = [at(f"yb{i}", M + kb, [P, TOPK, D]) for i, kb in enumerate([145, 165, 113])]
        pg_raw = [at(f"pg_raw{s}", M + 48 + 8 * s, [P, 2, D]) for s in range(4)]
        pg_lo = [at(f"pg_lo{s}", M + 48 + 8 * s, [P, 2, D], F32R) for s in range(4)]
        pg_hi = [at(f"pg_hi{s}", M + kb, [P, 2, D], F32R) for s, kb in enumerate([80, 88, 97, 105])]
        x_hi = at("x_hi", M, [P, TT, CT, P], F32R)
        x_lo = at("x_lo", M + 32, [P, TT, CT, P], F32R)
        gate = [at(f"gate{i}", M + 129 + 2 * i, [P, NCOL]) for i in range(2)]
        sq_out = at("sq_out", M + 133, [P, D])
        bdn = at("bdn", M + 137, [NE, D])
        wexp_T = at("wexp_T", M + 141, [NE, T])
        g_fin = at("g_fin", M + 161, [P, D])

        hf_rows = nc.dram_tensor("hf_rows", (T, D), F32, kind="Internal").ap()
        y_rows = nc.dram_tensor("y_rows", (T * TOPK, D), F32, kind="Internal").ap()

        x_in = [sem(f"x_in{i}") for i in range(TT)]
        par_in = sem("par_in")
        par_done = sem("par_done")
        par_ready = sem("par_ready")
        sq_own = sem("sq_own")
        rms_ready = sem("rms_ready")
        xn_ready = sem("xn_ready")
        turned = sem("turned")
        turned_hi = sem("turned_hi")
        turned_out = sem("turned_out")
        raw_in = [sem(f"raw_in{s}") for s in range(4)]
        hi_ready = sem("hi_ready")
        lo_ready = sem("lo_ready")
        gran_used = sem("gran_used")
        bank_done = sem("bank_done")
        bank_free = sem("bank_free")
        pad_done = sem("pad_done")
        cv_ready = sem("cv_ready")
        tap_ready = sem("tap_ready")
        tap_added = sem("tap_added")
        ls_ready = sem("ls_ready")
        ln_mean = sem("ln_mean")
        ln_cent = sem("ln_cent")
        ln_sq = sem("ln_sq")
        ln_sq_used = sem("ln_sq_used")
        ln_dev = sem("ln_dev")
        ln_rs = sem("ln_rs")
        ln_scaled = sem("ln_scaled")
        ln_z = sem("ln_z")
        ln_sig = sem("ln_sig")
        ln_val = sem("ln_val")
        ln_hi = sem("ln_hi")
        c_ready = sem("c_ready")
        gs_ready = sem("gs_ready")
        q_ready = sem("q_ready")
        k_ready = sem("k_ready")
        bexp_ready = sem("bexp_ready")
        bexp_done = sem("bexp_done")
        tab_in = sem("tab_in")
        eps_ready = sem("eps_ready")
        qkT_done = sem("qkT_done")
        qT_ready = sem("qT_ready")
        kT_ready = sem("kT_ready")
        sc_done = sem("sc_done")
        sT_ready = sem("sT_ready")
        out_done = sem("out_done")
        out_used = sem("out_used")
        dev_ready = sem("dev_ready")
        gated = sem("gated")
        st_done = sem("st_done")
        state_ready = sem("state_ready")
        mix_ready = sem("mix_ready")
        mix_hi = sem("mix_hi")
        mix_lo = sem("mix_lo")
        hf_out = sem("hf_out")
        lg_done = sem("lg_done")
        lg_ready = sem("lg_ready")
        exp_ready = sem("exp_ready")
        msk_ready = sem("msk_ready")
        rank_done = sem("rank_done")
        maxc_ready = sem("maxc_ready")
        oh_ready = sem("oh_ready")
        tab_done = sem("tab_done")
        tab_ready = sem("tab_ready")
        pass_done = sem("pass_done")
        w_in_s = [sem(f"w_in_s{s}") for s in range(SLOTS)]
        slot_used = sem("slot_used")
        idx_g_done = sem("idx_g_done")
        idx_s_done = sem("idx_s_done")
        gathered = sem("gathered")
        xt_done = sem("xt_done")
        xT_ready = sem("xT_ready")
        gu_done = sem("gu_done")
        z_ready = sem("z_ready")
        sg_ready = sem("sg_ready")
        act_ready = sem("act_ready")
        dn_hi_ready = sem("dn_hi_ready")
        dn_lo_ready = sem("dn_lo_ready")
        act_hi_ready = sem("act_hi_ready")
        act_lo_ready = sem("act_lo_ready")
        y_done = sem("y_done")
        yr_ready = sem("yr_ready")
        scattered = sem("scattered")
        rows_left = sem("rows_left")
        xg_zero = sem("xg_zero")
        moe_done = sem("moe_done")
        wexp_ready = sem("wexp_ready")
        experts_left = sem("experts_left")
        yb_in = [sem(f"yb_in{i}") for i in range(TT)]
        bdn_in = sem("bdn_in")
        wT_done = sem("wT_done")
        wT_ready = sem("wT_ready")
        bias_done = sem("bias_done")
        pg_hi_ready = sem("pg_hi_ready")
        pg_lo_ready = sem("pg_lo_ready")
        g_fin_in = sem("g_fin_in")
        x2_ready = sem("x2_ready")
        tail_in = sem("tail_in")
        pT_done = sem("pT_done")
        pT_ready = sem("pT_ready")
        lgT_done = sem("lgT_done")
        lgT_ready = sem("lgT_ready")
        pp_done = sem("pp_done")
        pp_ready = sem("pp_ready")
        x_turned = sem("x_turned")
        x_hi_ready = sem("x_hi_ready")
        x_lo_ready = sem("x_lo_ready")
        pg_done = sem("pg_done")
        gate_used = sem("gate_used")
        inv_ready = sem("inv_ready")
        gate_ready = sem("gate_ready")
        x3_ready = sem("x3_ready")
        fin_ready = sem("fin_ready")
        out_sem = sem("out_sem")
        dve_own = sem("dve_own")
        dve_moe = sem("dve_moe")
        dve_pass = sem("dve_pass")
        pool_own = sem("pool_own")
        sp_waited = sem("sp_waited")
        pool_waited = sem("pool_waited")

        pool_taps = [(kk, ct) for kk in range(1, TAPS) for ct in (2 * POOL_PAIR, 2 * POOL_PAIR + 1)]
        assert sum(map(sum, TAP_STEPS.values())) == len(pool_taps)

        def tap(kk, ct):
            r = kk * CT + ct
            return wdw[:, r // TAP_ROWS, r % TAP_ROWS:r % TAP_ROWS + 1]

        def col(first, ct):
            return par[:, first + ct:first + ct + 1]

        def rotate(engine, own, dst, table, b, a, s, done, queue):
            if b:
                queue.wait_ge(done, b)
            cos, sin = (rope[:, table + i, b, :].unsqueeze(1).unsqueeze(1).to_broadcast([P, HEADS, 2, HALF])
                        for i in range(2))
            own.mark(engine.tensor_tensor(a[:], dst[:, b], cos, ALU.mult))
            own.link(engine.tensor_tensor(s[:], dst[:, b], sin, ALU.mult))
            own.mark(engine.tensor_tensor(dst[:, b, :, 0, :], a[:, :, 0, :], s[:, :, 1, :], ALU.subtract))
            engine.tensor_tensor(dst[:, b, :, 1, :], a[:, :, 1, :], s[:, :, 0, :], ALU.add).then_inc(done, 1)

        w_granules = lambda w: w.rearrange("(s k p) n -> s p k n", k=2, p=P)
        win_g, wret_g, wconv_g, wo_g, wpg_g = map(w_granules, (t.w_in, t.w_ret_out, t.w_conv_out, t.w_o, t.w_ple_gate))
        PAR_DMAS, TAB_DMAS = 11, 8

        PAR_ROWS = ((t.g_mix, PR_MIX), (t.ret_gn_w, PR_GN), (t.b_dw, PR_BDW), (t.conv_ln_w, PR_LNW),
                    (t.conv_ln_b, PR_LNB), (t.b_conv_out, PR_BCO), (t.g_ffn, PR_FFN), (t.g_ple, PR_PLE))

        def load_rows(queue, vectors):
            for vec, first in vectors:
                queue.dma_start(rows[first:first + CT, 0, :], vec.rearrange("(c p) -> c p", p=P)).then_inc(par_in, 16)

        K_TURNED = {(10, 3): 0, (11, 2): 1, (12, 1): 2, (13, 0): 3}
        RET_TURNED = {(14, 1): (0, 1, 2, 3), (14, 3): (4, 5, 6, 7)}

        LN_STEPS = {(15, 3): (0, 1, 2, 3), (16, 0): (4,), (16, 1): (5,), (16, 3): (6, 7, 8, 9)}

        block = ctx.enter_context(nc.Block())

        @block.sync
        def _(sp):
            x_t = t.x.rearrange("(t p) d -> t p d", p=P)
            for i in range(TT):
                sp.dma_start(x[:, i, :], x_t[i]).then_inc(x_in[i], 16)

            def chunk(src, c, column):
                for s in range(4):
                    if not isinstance(c, int) or c > 0:
                        sp.wait_ge(lo_ready, 4 * (c - 1) + s + 1)
                    sp.dma_start(raw[s][:], src[s, :, :, bass.ds(column, NCOL)]).then_inc(raw_in[s], 16)

            sp.dma_start(ident[:], t.ident).then_inc(par_in, 16)
            load_rows(sp, PAR_ROWS[0:1] + PAR_ROWS[5:])
            taps = t.w_dw.rearrange("k (c p) -> (k c) p", p=P)
            for i in range(2):
                sp.dma_start(rows[0:TAP_ROWS, 1 + i, :], taps[i * TAP_ROWS:(i + 1) * TAP_ROWS]).then_inc(par_in, 16)
            chunk(win_g, 0, COL_GLU_B)
            chunk(win_g, 1, COL_GLU_A)
            chunk(win_g, 2, COL_GLU_B + NCOL)
            chunk(win_g, 3, COL_GLU_A + NCOL)
            with sp.Fori(0, CH_MC - CH_QK) as j:
                chunk(win_g, j + CH_QK, j * NCOL + COL_Q)
            with sp.Fori(0, 2) as j:
                chunk(win_g, j + CH_MC, j * NCOL + COL_MCONV)
            with sp.Fori(0, 2) as j:
                chunk(win_g, j + CH_MR, j * NCOL + COL_MRET)
            for first, src in ((CH_YR, wret_g), (CH_YC, wconv_g), (CH_WO, wo_g)):
                with sp.Fori(0, 2) as j:
                    chunk(src, j + first, j * NCOL)

            gu_w = t.w_gu.rearrange("e (s p) n -> e s p n", p=P)
            dn_w = t.w_down.rearrange("e (s k p) n -> e s p k n", k=2, p=P)

            def load_slot(e, s):
                if s < GU_SLOTS:
                    src = gu_w[bass.ds(e, 1), s].rearrange("o p n -> (o p) n")
                    dst = wslot[s][:]
                else:
                    src = dn_w[bass.ds(e, 1), s - GU_SLOTS].rearrange("o p k n -> (o p) k n")
                    dst = wslot[s][:].rearrange("p (k n) -> p k n", k=2)
                sp.dma_start(dst, src).then_inc(w_in_s[s], 16)

            def load_expert(n, e):
                for s in range(SLOTS):
                    if s == 7:
                        sp.wait_ge(gu_done, 4 * n)
                    elif s == 11:
                        sp.wait_ge(y_done, 2 * n)
                    else:
                        sp.wait_ge(slot_used, 10 * (n - 1) + (s + 1 if s < 7 else s))
                    load_slot(e, s)

            sp.wait_ge(bank_done, 4 * CH_YR)
            for s in range(4):
                load_slot(0, s)
            sp.wait_ge(mix_lo, CT)
            for s in range(4, SLOTS):
                load_slot(0, s)
            sp.wait_ge(lo_ready, 4 * CHUNKS)
            sp.dma_start(p_in[:], t.p.rearrange("(t p) d -> p t d", p=P)).then_inc(tail_in, 16)
            sp.dma_start(wpp[:], t.w_ple_proj.rearrange("(k p) n -> p k n", p=P)).then_inc(tail_in, 16)
            with sp.Fori(1, NE) as e:
                load_expert(e, e)
            sp.wait_ge(gu_done, 4 * NE)
            sp.wait_ge(maxc_ready, 1)
            fullest = sp.value_load(maxc[0:1, 0:1], min_val=0, max_val=T)
            with sp.If(fullest > CAP):
                with sp.Fori(1, PASSES) as m:
                    with sp.If(fullest > m * CAP):
                        with sp.Fori(0, NE) as e:
                            load_expert(m * NE + e, e)
                        sp.wait_ge(gu_done, m * 4 * NE + 4 * NE)
                        sp.sem_inc(sp_waited, 1)

            for s in range(4):
                sp.dma_start(pg_raw[s][:], wpg_g[s]).then_inc(raw_in[s], 16)
            sp.dma_start(bdn[:], t.b_down).then_inc(bdn_in, 16)
            sp.wait_ge(experts_left, 1)
            sp.wait_ge(moe_done, 1)
            y_t = y_rows.rearrange("(t p k) d -> t p k d", p=P, k=TOPK)
            for i in range(TT):
                if i >= 3:
                    sp.wait_ge(x2_ready, i - 2)
                sp.dma_start(yb[i % 3][:], y_t[i]).then_inc(yb_in[i], 16)
            sp.dma_start(g_fin[:], t.g_final.partition_broadcast(P)).then_inc(g_fin_in, 16)
            out_t = t.out.rearrange("(t p) d -> t p d", p=P)
            for i in range(TT):
                sp.wait_ge(fin_ready, i + 1)
                sp.dma_start(out_t[i], x[:, i, :]).then_inc(out_sem, 16)
            sp.wait_ge(out_sem, 16 * TT)

        def pe_chunk(pe, c, hi, lo, stationary, ready=None, after=None):
            for s in range(4):
                pe.wait_ge(lo_ready, 4 * c + s + 1)
                for kk in range(2):
                    kt = 2 * s + kk
                    if ready:
                        ready(kt)
                    for b in range(4):
                        if kt == 0 and (not isinstance(c, int) or c > 0):
                            pe.wait_ge(bank_free, 4 * (c - 1) + b + 1)
                        cols = slice(b * P, (b + 1) * P)
                        for i, (w, o) in enumerate(((whi, hi), (whi, lo), (wlo, hi))):
                            a = w[s][:, kk, cols] if stationary else o[:, kt, cols]
                            m = o[:, kt, :] if stationary else w[s][:, kk, :]
                            mm = nc.tensor.matmul(bank[b][:], a, m, start=(kt == 0 and i == 0),
                                                  stop=(kt == CT - 1 and i == 2))
                        if kt == CT - 1:
                            mm.then_inc(bank_done, 1)
                if s < 3:
                    mm.then_inc(gran_used, 1)
                if after:
                    after(s)

        def turn(pe, i, src, ct):
            if i >= 4:
                pe.wait_ge(turned_out, i - 3)
            for tt in range(TT):
                tr = nc.tensor.transpose(bank[4 + i % 4][:, tt * P:(tt + 1) * P],
                                         src[:, tt, ct * P:(ct + 1) * P], ident[:])
            tr.then_inc(turned, 1)

        @block.tensor
        def _(pe):
            pe.wait_ge(par_in, 16 * PAR_DMAS)
            nc.tensor.transpose(bank[4][:, 0:64], rows[0:64, 0, :], ident[0:64, 0:64])
            for i in range(2):
                tr = nc.tensor.transpose(bank[4][:, 64 + TAP_ROWS * i:64 + TAP_ROWS * (i + 1)],
                                         rows[0:TAP_ROWS, 1 + i, :], ident[0:TAP_ROWS, 0:TAP_ROWS])
            tr.then_inc(par_done, 1)
            pe.wait_ge(par_ready, 1)
            pe.wait_ge(xn_ready, TT)
            for ct in range(CT):
                turn(pe, ct, xn, ct)
            pe_chunk(pe, 0, h_hi, h_lo, True, ready=lambda kt: pe.wait_ge(turned_out, kt + 1))
            pe.wait_ge(tab_in, 16 * TAB_DMAS)
            for i in range(16):
                tr = nc.tensor.transpose(bank[4][:, i * NE:(i + 1) * NE], brow[:, i * P:(i + 1) * P],
                                         ident[0:NE, 0:NE])
            tr.then_inc(bexp_done, 1)
            with pe.Fori(1, CH_QK) as c:
                pe_chunk(pe, c, h_hi, h_lo, True)
            with pe.Fori(CH_QK, CH_MC) as c:
                pe_chunk(pe, c, h_hi, h_lo, False)

            def turn_qk(j):
                if j == 0:
                    pe.wait_ge(q_ready, TT)
                    pe.wait_ge(k_ready, TT)
                    pe.wait_ge(bexp_ready, 1)
                else:
                    pe.wait_ge(out_used, j)
                for h in range(HEADS):
                    nc.tensor.transpose(bank[4][:, h * P:(h + 1) * P],
                                        q[:, j, h].rearrange("p a b -> p (a b)"), ident[:])
                for h in range(HEADS):
                    tr = nc.tensor.transpose(bank[5][:, h * P:(h + 1) * P],
                                             k[:, j, h].rearrange("p a b -> p (a b)"), ident[:])
                tr.then_inc(qkT_done, 1)

            def scores(j):
                pe.wait_ge(qT_ready, j + 1)
                pe.wait_ge(kT_ready, j + 1)
                if j:
                    pe.wait_ge(state_ready, j)
                for h in range(HEADS):
                    mm = nc.tensor.matmul(bank[6][:, h * P:(h + 1) * P], k_T[:, h, :], q_T[:, h, :],
                                          start=True, stop=True)
                mm.then_inc(sc_done, 1)

            def outputs(j):
                pe.wait_ge(sT_ready, j + 1)
                for h in range(HEADS):
                    o = bank[4 + h // 2][:, (h % 2) * DV:(h % 2 + 1) * DV]
                    mm = nc.tensor.matmul(o, s_T[:, h, :], v[:, j, h * DV:(h + 1) * DV], start=True, stop=(j == 0))
                    if j:
                        mm = nc.tensor.matmul(o, qd_T[:, h, :], state[:, h, :], start=False, stop=True)
                mm.then_inc(out_done, 1)
                if j < TT - 1:
                    for h in range(HEADS):
                        mm = nc.tensor.matmul(bank[6 + h // 2][:, (h % 2) * DV:(h % 2 + 1) * DV], kd[:, h, :],
                                              v[:, j, h * DV:(h + 1) * DV], start=True, stop=True)
                    mm.then_inc(st_done, 1)

            steps = {(10, 0): (turn_qk, 0), (10, 1): (scores, 0), (10, 2): (outputs, 0), (10, 3): (turn_qk, 1),
                     (11, 0): (scores, 1), (11, 1): (outputs, 1), (11, 2): (turn_qk, 2), (11, 3): (scores, 2),
                     (12, 0): (outputs, 2), (12, 1): (turn_qk, 3), (12, 2): (scores, 3), (12, 3): (outputs, 3)}

            def retention(c):
                def after(s):
                    if (c, s) in steps:
                        f, j = steps[c, s]
                        f(j)
                return after

            for c in range(CH_MC, CH_MR + 1):
                pe_chunk(pe, c, h_hi, h_lo, True, after=retention(c))

            def turn_ret(s):
                if s == 2:
                    pe.wait_ge(gated, 1)
                for ct in {2: (0, 1, 2, 3), 3: (4, 5, 6, 7)}.get(s, ()):
                    turn(pe, CT + ct, g, ct)

            pe_chunk(pe, CH_MR + 1, h_hi, h_lo, True, after=turn_ret)

            def layer_norm(c):
                def after(s):
                    if (c, s) == (CH_YR, 1):
                        pe.wait_ge(ls_ready, 1)
                        pe.wait_ge(turned_out, CT + 5)
                        nc.tensor.matmul(bank[4][:], ones[:], lsum[:], start=True, stop=True).then_inc(ln_mean, 1)
                    if (c, s) == (CH_YR, 3):
                        for ct in range(CT):
                            pe.wait_ge(ln_sq, ct + 1)
                            nc.tensor.matmul(bank[5][:], ones[:], sq[ct % 2][:], start=(ct == 0),
                                             stop=(ct == CT - 1)).then_inc(ln_sq_used, 1)
                return after

            pe_chunk(pe, CH_YR, r_hi, r_lo, True, ready=lambda kt: pe.wait_ge(turned_out, CT + kt + 1),
                     after=layer_norm(CH_YR))
            pe_chunk(pe, CH_YR + 1, r_hi, r_lo, True)
            pe_chunk(pe, CH_YC, c_hi, c_lo, True, ready=lambda kt: pe.wait_ge(c_ready, kt + 1))
            pe_chunk(pe, CH_YC + 1, c_hi, c_lo, True)

            def mixed_ready(kt):
                pe.wait_ge(mix_lo, kt + 1)
            pe_chunk(pe, CH_WO, mx_hi, mx_lo, False, ready=mixed_ready)
            pe_chunk(pe, CH_WO + 1, mx_hi, mx_lo, False)

            pe.wait_ge(bank_free, 4 * CHUNKS)
            for ct in range(CT):
                turn(pe, 2 * CT + ct, x, ct)
            for ct in range(CT):
                pe.wait_ge(turned_out, 2 * CT + ct + 1)
                mm = nc.tensor.matmul(bank[0][0:NE, :], w_rout[:, ct, :], f_T[:, ct, :],
                                      start=(ct == 0), stop=(ct == CT - 1))
            mm.then_inc(lgT_done, 1)
            pe.wait_ge(lgT_ready, 1)
            for tt in range(TT):
                tr = nc.tensor.transpose(bank[0][:, tt * NE:(tt + 1) * NE], lg_T[:, tt * P:(tt + 1) * P],
                                         ident[0:NE, 0:NE])
            tr.then_inc(lg_done, 1)
            pe.wait_ge(tail_in, 32)
            for kt in range(2):
                for tt in range(TT):
                    tr = nc.tensor.transpose(bank[2 + kt][:, tt * P:(tt + 1) * P], p_in[:, tt, kt * P:(kt + 1) * P],
                                             ident[:])
            tr.then_inc(pT_done, 1)

            def embed(tiles):
                for i in tiles:
                    tt, n2 = i // 2, i % 2
                    if i >= 2:
                        pe.wait_ge(pp_ready, i - 1)
                    for kt in range(2):
                        mm = nc.tensor.matmul(bank[2 + i % 2][:], p_T[:, kt, tt * P:(tt + 1) * P],
                                              wpp[:, kt, n2 * NCOL:(n2 + 1) * NCOL], start=(kt == 0), stop=(kt == 1))
                    mm.then_inc(pp_done, 1)

            pe.wait_ge(pT_ready, 1)
            embed(range(0, 1))
            pe.wait_ge(msk_ready, 1)
            for tt in range(TT + 1):
                for j in range(min(tt, TT - 1) + 1):
                    mm = nc.tensor.matmul(bank[1][:, tt * NE:(tt + 1) * NE], tri[:] if j == tt else ones[:],
                                          msk[:, j, :], start=(j == 0), stop=(j == min(tt, TT - 1)))
            mm.then_inc(rank_done, 1)
            embed(range(1, 3))

            def turn_x(c):
                pe.wait_ge(gathered, 16 * (c + 1))
                for kt in range(CT):
                    tr = nc.tensor.transpose(bank[6 + kt // 4][:, (kt % 4) * CAP:(kt % 4 + 1) * CAP],
                                             xg[0:CAP, kt * P:(kt + 1) * P], ident[0:CAP, 0:CAP])
                    if kt % 4 == 3:
                        tr.then_inc(xt_done, 1)

            def expert(n, c):
                pe.wait_ge(xT_ready, 2 * c + 2)
                def gate_up(s, b):
                    for i in range(4):
                        mt = 2 * b + i % 2 + CT * (i // 2)
                        mm = nc.tensor.matmul(bank[b][:, i * CAP:(i + 1) * CAP], wslot[s][:, mt * P:(mt + 1) * P],
                                              x_T[:, s, :], start=(s == 0 and i == 0), stop=(s == GU_SLOTS - 1),
                                              skip_group_check=True)
                    return mm

                for s in range(GU_SLOTS - 2):
                    pe.wait_ge(w_in_s[s], 16 * (n + 1))
                    for b in range(4):
                        mm = gate_up(s, b)
                    mm.then_inc(slot_used, 1)
                for s in (GU_SLOTS - 2, GU_SLOTS - 1):
                    pe.wait_ge(w_in_s[s], 16 * (n + 1))
                for b in range(4):
                    mm = gate_up(GU_SLOTS - 2, b)
                    if b == 3:
                        mm.then_inc(slot_used, 1)
                    gate_up(GU_SLOTS - 1, b).then_inc(gu_done, 1)
                turn_x(c + 1)
                pe.wait_ge(yr_ready, 2 * n + 2)
                for r in range(4):
                    pe.wait_ge(dn_lo_ready, 4 * n + r + 1)
                    pe.wait_ge(act_lo_ready, 4 * n + r + 1)
                    for kk in range(2):
                        kt = 2 * r + kk
                        for i, (a, w) in enumerate(((act_hi, dn_hi[r]), (act_hi, dn_lo[r]), (act_lo, dn_hi[r]))):
                            for n2 in range(2):
                                mm = nc.tensor.matmul(bank[4 + n2][0:CAP, :], a[:, kt, :],
                                                      w[:, kk * D + n2 * NCOL:kk * D + (n2 + 1) * NCOL],
                                                      start=(kt == 0 and i == 0), stop=(kt == CT - 1 and i == 2))
                                if kt == CT - 1 and i == 2:
                                    mm.then_inc(y_done, 1)
                    if r < 3:
                        mm.then_inc(slot_used, 1)

            def tables(m):
                pe.wait_ge(oh_ready, m + 1)
                for i in range(TT * TOPK):
                    mm = nc.tensor.matmul(bank[4][0:CAP, 0:2 * NE], oha[:, i // TOPK, i % TOPK, :],
                                          ohb[:, i // TOPK, i % TOPK].rearrange("p w e -> p (w e)"),
                                          start=(i == 0), stop=(i == TT * TOPK - 1))
                mm.then_inc(tab_done, 1)

            def pass_end(passes):
                pe.wait_ge(xT_ready, passes * 2 * (NE + 1))
                pe.wait_ge(yr_ready, passes * 2 * NE + 2)

            tables(0)
            embed(range(3, 2 * TT))
            turn_x(0)
            pe.wait_ge(pp_ready, 2 * TT)
            with pe.Fori(0, NE) as e:
                expert(e, e)
            pass_end(1)
            pe.wait_ge(maxc_ready, 1)
            fullest = pe.value_load(maxc[0:1, 0:1], min_val=0, max_val=T)
            with pe.If(fullest > CAP):
                with pe.Fori(1, PASSES) as m:
                    with pe.If(fullest > m * CAP):
                        tables(m)
                        turn_x(m * (NE + 1))
                        with pe.Fori(0, NE) as e:
                            expert(m * NE + e, m * (NE + 1) + e)
                        pass_end(m + 1)
            pe.sem_inc(experts_left, 1)

            pe.wait_ge(wexp_ready, 1)
            for tt in range(TT):
                tr = nc.tensor.transpose(bank[6][0:NE, tt * P:(tt + 1) * P], wexp[:, tt, :], ident[:])
            tr.then_inc(wT_done, 1)
            pe.wait_ge(wT_ready, 1)
            pe.wait_ge(bdn_in, 16)
            for i in range(2 * TT):
                nc.tensor.matmul(bank[(i + 4) % 8][:], wexp_T[:, (i // 2) * P:(i // 2 + 1) * P],
                                 bdn[:, (i % 2) * NCOL:(i % 2 + 1) * NCOL], start=True, stop=True).then_inc(bias_done, 1)

            def turn_tile(tt):
                pe.wait_ge(x2_ready, tt + 1)
                if tt >= 2:
                    pe.wait_ge(x_lo_ready, 2 * tt - 2)
                for ct in range(CT):
                    tr = nc.tensor.transpose(bank[4 + 2 * (tt % 2) + ct // 4][:, (ct % 4) * P:(ct % 4 + 1) * P],
                                             x[:, tt, ct * P:(ct + 1) * P], ident[:])
                    if ct % 4 == 3:
                        tr.then_inc(x_turned, 1)

            def gate_product(tt, n2):
                if tt >= 2:
                    pe.wait_ge(gate_ready, 2 * (tt - 2) + n2 + 1)
                cols = slice(n2 * NCOL, (n2 + 1) * NCOL)
                for kt in range(CT):
                    s, kk = kt // 2, kt % 2
                    if tt == 0:
                        pe.wait_ge(pg_lo_ready, kt + 1)
                    if kt % 4 == 0:
                        pe.wait_ge(x_lo_ready, 2 * tt + kt // 4 + 1)
                    for i, (a, w) in enumerate(((x_hi, pg_hi), (x_hi, pg_lo), (x_lo, pg_hi))):
                        mm = nc.tensor.matmul(bank[2 * (tt % 2) + n2][:], a[:, tt, kt, :], w[s][:, kk, cols],
                                              start=(kt == 0 and i == 0), stop=(kt == CT - 1 and i == 2))
                mm.then_inc(pg_done, 1)

            turn_tile(0)
            turned_behind = {(0, 0): 1, (1, 0): 2, (2, 0): 3}
            for tt in range(TT):
                for n2 in range(2):
                    gate_product(tt, n2)
                    if (tt, n2) in turned_behind:
                        turn_tile(turned_behind[tt, n2])

        @block.scalar
        def _(act):
            load_rows(act, PAR_ROWS[1:5])

            sq_chain = Chain(act, sq_own)

            def root_mean_squares(first, wait, out):
                for tt in range(TT):
                    wait(tt)
                    last = sq_chain.mark(nc.scalar.activation(out(tt), x[:, tt, :], ACT.Square,
                                                              accum_out=ss[:, first + tt:first + tt + 1]))
                act.wait_ge(eps_ready, 1)
                sq_chain.wait(last)
                group = ss[:, first:first + TT]
                nc.scalar.activation(group, group, ACT.Sqrt, bias=eps, scale=1.0 / D).then_inc(rms_ready, 1)

            root_mean_squares(0, lambda tt: act.wait_ge(x_in[tt], 16), lambda tt: xn[:, tt, :])

            def hi_part(c, s):
                act.wait_ge(raw_in[s], 16 * (c + 1))
                if c:
                    if s < 3:
                        act.wait_ge(gran_used, 3 * (c - 1) + s + 1)
                    else:
                        act.wait_ge(bank_done, 4 * c)
                nc.scalar.copy(whi[s][:], raw[s][:]).then_inc(hi_ready, 1)

            def turned_hi_part(i, hi, first, ct):
                act.wait_ge(turned, i + 1)
                nc.scalar.activation(hi[:, ct, :], bank[4 + i % 4][:], ACT.Copy,
                                     scale=col(first, ct)).then_inc(turned_hi, 1)

            def sigmoid_tile(c, b, out, done=bank_free):
                act.wait_ge(bank_done, 4 * c + b + 1)
                nc.scalar.activation(out, bank[b][:], ACT.Sigmoid).then_inc(done, 1)

            def k_turned(j):
                act.wait_ge(qkT_done, j + 1)
                nc.scalar.copy(k_T[:], bank[5][:].rearrange("p (h c) -> p h c", h=HEADS)).then_inc(kT_ready, 1)

            def evac(c):
                if c in (0, 2):
                    if c == 2:
                        act.wait_ge(bank_free, 8)
                    for b in range(4):
                        sigmoid_tile(c, b, sgb[:, b, :])
                elif c in (4, 5):
                    for b in range(4):
                        act.wait_ge(bank_done, 4 * c + b + 1)
                        nc.scalar.copy((q, k)[c - 4][:, b].rearrange("p h a r -> p (h a r)"),
                                       bank[b][:]).then_inc(bank_free, 1)
                elif c in (6, 7):
                    for b in range(4):
                        act.wait_ge(bank_done, 4 * c + b + 1)
                        nc.scalar.copy(v[:, b, (c - 6) * NCOL:(c - 5) * NCOL], bank[b][:]).then_inc(bank_free, 1)
                elif c in (8, 9):
                    if c == 8:
                        act.wait_ge(k_ready, TT)
                    for b in range(4):
                        if 4 * (c - 8) + b >= 2:
                            act.wait_ge(bank_free, 4 * c + b - 1)
                        sigmoid_tile(c, b, gs[b % 2][:], gs_ready)
                elif c in (10, 11):
                    if c == 10:
                        act.wait_ge(cv_ready, 2)
                    else:
                        act.wait_ge(cv_ready, len(DVE_PAIRS))
                        act.wait_ge(tap_added, len(pool_taps))
                    for b in range(4):
                        sigmoid_tile(c, b, sm_c[:, 4 * (c - 10) + b, :])
                elif c in (12, 13):
                    if c == 12:
                        act.wait_ge(sc_done, TT)
                    else:
                        act.wait_ge(out_used, TT)
                    for b in range(4):
                        sigmoid_tile(c, b, sm_r[:, 4 * (c - 12) + b, :])
                elif c in (16, 17):
                    for b in range(4):
                        i = 4 * (c - 16) + b
                        act.wait_ge(mix_ready, i + 1)
                        nc.scalar.copy(mx_hi[:, i, :], sm_c[:, i, :]).then_inc(mix_hi, 1)

            hi_part(0, 0)
            act.wait_ge(par_ready, 1)
            for ct in range(CT):
                turned_hi_part(ct, h_hi, PR_MIX, ct)
            for s in range(1, 4):
                hi_part(0, s)

            tap_steps = range(len(pool_taps))
            for c in range(1, CHUNKS):
                for s in range(4):
                    if s == 3:
                        evac(c - 1)
                    hi_part(c, s)
                    for i in tap_steps[:TAP_STEPS[c][s]] if s < len(TAP_STEPS.get(c, ())) else ():
                        kk, ct = pool_taps[i]
                        if i >= 3:
                            act.wait_ge(tap_added, i - 2)
                        else:
                            act.wait_ge(bank_free, 16)
                        nc.scalar.activation(tapped[i % 3][:], cin[:, ct, kk:kk + T], ACT.Copy,
                                             scale=tap(kk, ct)).then_inc(tap_ready, 1)
                        tap_steps = tap_steps[1:]
                    if (c, s) == (15, 2):
                        for ct in range(CT):
                            act.wait_ge(ln_cent, ct + 1)
                            if ct >= 2:
                                act.wait_ge(ln_sq_used, ct - 1)
                            nc.scalar.square(sq[ct % 2][:], cv[:, ct, :]).then_inc(ln_sq, 1)
                    if (c, s) == (15, 3):
                        act.wait_ge(ln_sq_used, CT)
                        nc.scalar.activation(lrs[:], bank[5][:], ACT.Sqrt, bias=eps, scale=1.0 / D).then_inc(ln_dev, 1)
                    for i in LN_STEPS.get((c, s), ()):
                        if i < CT:
                            act.wait_ge(ln_z, i + 1)
                            if i >= 2:
                                act.wait_ge(ln_val, i - 1)
                            nc.scalar.activation(lsg[i % 2][:], cv[:, i, :], ACT.Sigmoid).then_inc(ln_sig, 1)
                        if 1 <= i <= CT:
                            act.wait_ge(ln_val, i)
                            nc.scalar.copy(c_hi[:, i - 1, :], cv[:, i - 1, :]).then_inc(ln_hi, 1)
                    if (c, s) in K_TURNED:
                        if c == 10:
                            act.wait_ge(tap_added, len(pool_taps))
                        k_turned(K_TURNED[c, s])
                    for ct in RET_TURNED.get((c, s), ()):
                        turned_hi_part(CT + ct, r_hi, PR_GN, ct)
                if c == 13:
                    act.wait_ge(out_used, TT)
                    nc.scalar.activation(mv[:, :, :, 1], mv[:, :, :, 1], ACT.Sqrt, bias=eps).then_inc(dev_ready, 1)
            for ct in range(CT):
                i = 2 * CT + ct
                act.wait_ge(turned, i + 1)
                nc.scalar.activation(f_T[:, ct, :], bank[4 + i % 4][:], ACT.Copy,
                                     scale=col(PR_FFN, ct)).then_inc(turned_out, 1)
            root_mean_squares(0, lambda tt: act.wait_ge(bank_free, 4 * (CHUNKS - 1) + tt + 1), lambda tt: xn2[:, tt, :])

            def embedded(tiles):
                for i in tiles:
                    act.wait_ge(pp_done, i + 1)
                    nc.scalar.copy(pp[:, i // 2, (i % 2) * NCOL:(i % 2 + 1) * NCOL],
                                   bank[2 + i % 2][:]).then_inc(pp_ready, 1)

            act.wait_ge(lgT_done, 1)
            nc.scalar.copy(lg_T[:], bank[0][0:NE, :]).then_inc(lgT_ready, 1)
            act.wait_ge(pT_done, 1)
            for kt in range(2):
                ins = nc.scalar.copy(p_T[:, kt, :], bank[2 + kt][:])
            ins.then_inc(pT_ready, 1)
            embedded(range(0, 1))
            act.wait_ge(lg_ready, 1)
            for tt in range(TT):
                nc.scalar.activation(wtop[:, tt, :], top[:, tt, 0:TOPK], ACT.Exp,
                                     bias=nmax[:, tt:tt + 1]).then_inc(exp_ready, 1)

            embedded(range(1, 2 * TT))
            act.wait_ge(hf_out, 16 * TT)

            def expert(n):
                for r in range(4):
                    act.wait_ge(w_in_s[GU_SLOTS + r], 16 * (n + 1))
                    nc.scalar.copy(dn_hi[r][:], wslot[GU_SLOTS + r][:]).then_inc(dn_hi_ready, 1)
                for i in range(5):
                    if i < 4:
                        act.wait_ge(z_ready, 4 * n + i + 1)
                        nc.scalar.activation(sg[i % 2][:], z[i % 2][:, 0], ACT.Sigmoid,
                                             scale=ALPHA).then_inc(sg_ready, 1)
                    if i >= 1:
                        act.wait_ge(act_ready, 4 * n + i + 2)
                        pair = slice(2 * i - 2, 2 * i)
                        nc.scalar.copy(act_hi[:, pair, :], act_T[:, pair, :]).then_inc(act_hi_ready, 1)
                act.wait_ge(rows_left, n + 1)
                for j in range(2):
                    act.wait_ge(y_done, 2 * n + j + 1)
                    nc.scalar.copy(yr[0:CAP, j * NCOL:(j + 1) * NCOL], bank[4 + j][0:CAP, :]).then_inc(yr_ready, 1)

            with act.Fori(0, NE) as e:
                expert(e)
            act.wait_ge(maxc_ready, 1)
            fullest = act.value_load(maxc[0:1, 0:1], min_val=0, max_val=T)
            with act.If(fullest > CAP):
                with act.Fori(1, PASSES) as m:
                    with act.If(fullest > m * CAP):
                        with act.Fori(0, NE) as e:
                            expert(m * NE + e)

            for kt in range(CT):
                s, kk = kt // 2, kt % 2
                if kk == 0:
                    act.wait_ge(raw_in[s], 16 * (CHUNKS + 1))
                nc.scalar.activation(pg_hi[s][:, kk, :], pg_raw[s][:, kk, :], ACT.Copy,
                                     scale=col(PR_PLE, kt)).then_inc(pg_hi_ready, 1)

            def square(tt, first):
                sq_chain.link(nc.scalar.activation(sq_out[:], x[:, tt, :], ACT.Square,
                                                   accum_out=ss[:, first + tt:first + tt + 1]))

            def rms(first, last):
                nc.scalar.activation(ss[:, first:last], ss[:, first:last], ACT.Sqrt, bias=eps,
                                     scale=1.0 / D).then_inc(rms_ready, 1)

            def take_x(tt):
                for j in range(2):
                    act.wait_ge(x_turned, 2 * tt + j + 1)
                    nc.scalar.copy(x_hi[:, tt, 4 * j:4 * j + 4, :], bank[4 + 2 * (tt % 2) + j][:]
                                   .rearrange("p (c t) -> p c t", t=P)).then_inc(x_hi_ready, 1)
                square(tt, 0)

            def gate_sigmoid(tt, n2):
                i = 2 * tt + n2
                if i >= 2:
                    act.wait_ge(x3_ready, i - 1)
                act.wait_ge(pg_done, i + 1)
                nc.scalar.activation(gate[n2][:], bank[2 * (tt % 2) + n2][:], ACT.Sigmoid,
                                     scale=ss[:, tt:tt + 1]).then_inc(gate_ready, 1)

            def gate_tile(tt):
                for n2 in range(2):
                    gate_sigmoid(tt, n2)

            def square_final(tt):
                act.wait_ge(x3_ready, 2 * tt + 2)
                square(tt, TT)

            take_x(0)
            take_x(1)
            rms(0, 2)
            act.wait_ge(inv_ready, 1)
            gate_tile(0)
            take_x(2)
            gate_tile(1)
            square_final(0)
            take_x(3)
            rms(2, TT)
            act.wait_ge(inv_ready, 2)
            gate_tile(2)
            square_final(1)
            rms(TT, TT + 2)
            gate_tile(3)
            square_final(2)
            sq_chain.link(nc.scalar.activation(sq_out[:, 0:1], eps, ACT.Sqrt))
            square_final(3)
            rms(TT + 2, 2 * TT)

        @block.gpsimd
        def _(pool):
            nc.gpsimd.memset(ones[:], 1.0).then_inc(pad_done, 1)
            nc.gpsimd.memset(cin[:, :, 0:TAPS - 1], 0.0).then_inc(pad_done, 1)
            nc.gpsimd.memset(tok_tab[:, NE:NE + 1], EMPTY).then_inc(pad_done, 1)
            nc.gpsimd.memset(eps, EPS).then_inc(eps_ready, 1)
            pool.dma_start(brow[:], t.b_gu).then_inc(tab_in, 16)
            pool.dma_start(cst[:, 0:164], t.cst[:, 0:164]).then_inc(tab_in, 16)
            pool.dma_start(tri[:], t.tri).then_inc(tab_in, 16)
            pool.dma_start(rope[:], t.rope.rearrange("p (a t h) -> p a t h", a=4, t=TT)).then_inc(tab_in, 16)
            pool.dma_start(dmask[:], t.dmask.rearrange("p (h c) -> p h c", h=HEADS)).then_inc(tab_in, 16)
            pool.dma_start(dq[:], t.dq.rearrange("p (h c) -> p h c", h=HEADS)).then_inc(tab_in, 16)
            pool.dma_start(w_rout[:], t.w_router.rearrange("(c p) e -> p c e", p=P)).then_inc(tab_in, 16)
            pool.dma_start(b_rout[:], t.b_router.partition_broadcast(P)).then_inc(tab_in, 16)

            own = Chain(pool, pool_own)

            def add_taps(steps):
                for i in steps:
                    kk, ct = pool_taps[i]
                    pool.wait_ge(tap_ready, i + 1)
                    if i >= 2:
                        pool.wait_ge(tap_added, i - 1)
                    nc.gpsimd.tensor_tensor(cv[:, ct, :], cv[:, ct, :], tapped[i % 3][:], ALU.add).then_inc(tap_added, 1)

            pool.wait_ge(bank_free, 16)
            pool.wait_ge(pad_done, 2)
            for ct in (2 * POOL_PAIR, 2 * POOL_PAIR + 1):
                own.link(nc.gpsimd.tensor_scalar(cv[:, ct, :], cin[:, ct, 0:T], tap(0, ct), col(PR_BDW, ct),
                                                 ALU.mult, ALU.add))
            before_k = sum(sum(n) for c, n in TAP_STEPS.items() if c < CH_V + 1)
            add_taps(range(before_k))
            for b in range(TT):
                pool.wait_ge(bank_free, 4 * (CH_QK + 1) + b + 1)
                rotate(nc.gpsimd, own, k, 2, b, rot_pa, rot_pb, k_ready, pool)
            add_taps(range(before_k, len(pool_taps)))
            pool.wait_ge(cv_ready, len(DVE_PAIRS))
            pool.wait_ge(tap_added, len(pool_taps))
            pool.wait_ge(out_used, TT)
            own.link(nc.gpsimd.tensor_tensor(lsum[:], cv[:, 0, :], cv[:, 1, :], ALU.add))
            for ct in range(2, CT - 1):
                own.link(nc.gpsimd.tensor_tensor(lsum[:], lsum[:], cv[:, ct, :], ALU.add))
            nc.gpsimd.tensor_tensor(lsum[:], lsum[:], cv[:, CT - 1, :], ALU.add).then_inc(ls_ready, 1)

            pool.wait_ge(ln_rs, 1)
            for ct in range(CT):
                nc.gpsimd.tensor_tensor(cv[:, ct, :], cv[:, ct, :], lrs[:], ALU.mult).then_inc(ln_scaled, 1)

            hf_t = hf_rows.rearrange("(t p) d -> t p d", p=P)
            for tt in range(TT):
                pool.wait_ge(xn_ready, TT + tt + 1)
                pool.dma_start(hf_t[tt], xn2[:, tt, :]).then_inc(hf_out, 16)
            pool.wait_ge(rank_done, 1)
            nc.gpsimd.memset(xg[:], 0.0).then_inc(xg_zero, 1)
            pool.wait_ge(xg_zero, 1)
            pool.wait_ge(hf_out, 16 * TT)

            def wait_reg(sem, value):
                pool.wait_ge(sem, value)
                pool.sem_inc(pool_waited, 1)

            def gather(c, e):
                wait_reg(xt_done, 2 * c + 2)
                nc.gpsimd.tensor_copy(idx_g[0:CAP, :], tok_tab[0:CAP, bass.ds(e, 1)]).then_inc(idx_g_done, 1)
                wait_reg(idx_g_done, c + 1)
                nc.gpsimd.indirect_dma_start(
                    xg[0:CAP, :], None, hf_rows, bass.IndirectOffsetOnAxis(ap=idx_g[0:CAP, 0:1], axis=0),
                    bounds_check=T - 1, oob_is_err=False).then_inc(gathered, 16)

            def scatter(n, e):
                nc.gpsimd.tensor_copy(idx_s[0:CAP, :], asg_tab[0:CAP, bass.ds(e, 1)]).then_inc(idx_s_done, 1)
                wait_reg(idx_s_done, n + 1)
                wait_reg(yr_ready, 2 * n + 4)
                nc.gpsimd.indirect_dma_start(
                    y_rows, bass.IndirectOffsetOnAxis(ap=idx_s[0:CAP, 0:1], axis=0), yr[0:CAP, :], None,
                    bounds_check=T * TOPK - 1, oob_is_err=False).then_inc(scattered, 16)
                wait_reg(scattered, 16 * n + 16)
                pool.sem_inc(rows_left, 1)

            def one_pass(m):
                wait_reg(tab_ready, m + 1)
                gather(m * (NE + 1), 0)
                with pool.Fori(0, NE) as e:
                    gather(m * (NE + 1) + e + 1, e + 1)
                    scatter(m * NE + e, e)
                pool.sem_inc(pass_done, 1)

            one_pass(0)
            pool.wait_ge(maxc_ready, 1)
            fullest = pool.value_load(maxc[0:1, 0:1], min_val=0, max_val=T)
            with pool.If(fullest > CAP):
                with pool.Fori(1, PASSES) as m:
                    with pool.If(fullest > m * CAP):
                        one_pass(m)
            pool.sem_inc(moe_done, 1)

        @block.vector
        def _(dve):
            dve.sem_inc(act_ready, 2)
            dve.sem_inc(yr_ready, 2)
            dve.sem_inc(rows_left, 1)
            dve.sem_inc(xt_done, 2)
            own = Chain(dve, dve_own)
            V = nc.vector

            def inverse_rms(group, first, last):
                dve.wait_ge(rms_ready, group + 1)
                own.link(V.reciprocal(ss[:, first:last], ss[:, first:last]))

            def lo_part(c, s):
                dve.wait_ge(hi_ready, 4 * c + s + 1)
                V.tensor_tensor(wlo[s][:], raw[s][:], whi[s][:].bitcast(F32), ALU.subtract).then_inc(lo_ready, 1)

            def turned_lo_part(i, hi_count, hi, lo, first, ct):
                dve.wait_ge(turned_hi, hi_count)
                V.scalar_tensor_tensor(lo[:, ct, :], bank[4 + i % 4][:], col(first, ct), hi[:, ct, :].bitcast(F32),
                                       ALU.mult, ALU.subtract).then_inc(turned_out, 1)

            inverse_rms(0, 0, TT)
            for tt in range(TT):
                V.tensor_scalar(xn[:, tt, :], x[:, tt, :], ss[:, tt:tt + 1], None, ALU.mult).then_inc(xn_ready, 1)
            dve.wait_ge(par_done, 1)
            V.tensor_copy(par[:], bank[4][:, 0:64])
            V.tensor_copy(wdw[:].rearrange("p a r -> p (a r)"),
                          bank[4][:, 64:64 + 2 * TAP_ROWS]).then_inc(par_ready, 1)
            dve.wait_ge(par_ready, 1)
            lo_part(0, 0)
            for ct in range(CT):
                turned_lo_part(ct, ct + 1, h_hi, h_lo, PR_MIX, ct)
            for s in range(1, 4):
                lo_part(0, s)

            last_tap = {}
            conv_steps = [(pair, kk, ct) for pair in DVE_PAIRS for kk in range(TAPS) for ct in (2 * pair, 2 * pair + 1)]
            assert 4 * sum(CONV_STEPS.values()) + CONV_START >= len(conv_steps)

            def conv(steps):
                for pair, kk, ct in steps:
                    if kk == 0 and ct % 2 == 0:
                        dve.wait_ge(bank_free, 8 if pair < 2 else 16)
                        dve.wait_ge(pad_done, 2)
                    if kk == 0:
                        ins = V.tensor_scalar(cv[:, ct, :], cin[:, ct, 0:T], tap(0, ct), col(PR_BDW, ct),
                                              ALU.mult, ALU.add)
                    else:
                        own.wait(last_tap[ct])
                        ins = V.scalar_tensor_tensor(cv[:, ct, :], cin[:, ct, kk:kk + T], tap(kk, ct),
                                                     cv[:, ct, :], ALU.mult, ALU.add)
                    if kk == TAPS - 1 and ct % 2:
                        ins.then_inc(cv_ready, 1)
                    else:
                        last_tap[ct] = own.mark(ins)

            def evac(c):
                for b in range(4):
                    def done():
                        dve.wait_ge(bank_done, 4 * c + b + 1)
                    if c in (1, 3):
                        done()
                        V.tensor_tensor(cin[:, 2 * (c - 1) + b, TAPS - 1:], bank[b][:], sgb[:, b, :],
                                        ALU.mult).then_inc(bank_free, 1)
                    elif c in (8, 9):
                        dve.wait_ge(gs_ready, 4 * (c - 8) + b + 1)
                        V.tensor_tensor(g[:, b, (c - 8) * NCOL:(c - 7) * NCOL], bank[b][:], gs[b % 2][:],
                                        ALU.mult).then_inc(bank_free, 1)
                    elif c in (14, 15):
                        i = 4 * (c - 14) + b
                        done()
                        V.tensor_tensor(sm_r[:, i, :], bank[b][:], sm_r[:, i, :], ALU.mult).then_inc(bank_free, 1)
                    elif c in (16, 17):
                        i = 4 * (c - 16) + b
                        done()
                        V.scalar_tensor_tensor(sm_c[:, i, :], bank[b][:], col(PR_BCO, i), sm_c[:, i, :],
                                               ALU.add, ALU.mult).then_inc(bank_free, 1)
                    elif c in (18, 19):
                        done()
                        xs = x[:, b, (c - 18) * NCOL:(c - 17) * NCOL]
                        V.tensor_tensor(xs, bank[b][:], xs, ALU.add).then_inc(bank_free, 1)
                if c in (16, 17):
                    tiles = range(4 * (c - 16), 4 * (c - 16) + 4)
                    for i in tiles:
                        dve.wait_ge(bank_free, 4 * 16 + i + 1)
                        V.tensor_tensor(sm_c[:, i, :], sm_c[:, i, :], sm_r[:, i, :], ALU.add).then_inc(mix_ready, 1)
                    for i in tiles:
                        dve.wait_ge(mix_hi, i + 1)
                        V.tensor_tensor(mx_lo[:, i, :], sm_c[:, i, :], mx_hi[:, i, :].bitcast(F32),
                                        ALU.subtract).then_inc(mix_lo, 1)

            def turned_qk(j):
                if j == 0:
                    dve.wait_ge(tap_added, len(pool_taps))
                dve.wait_ge(qkT_done, j + 1)
                src = bank[4][:].rearrange("p (h c) -> p h c", h=HEADS)
                V.tensor_copy(q_T[:], src)
                if j < TT - 1:
                    V.tensor_tensor(kd[:], k[:, j].rearrange("p h a r -> p h (a r)"),
                                    dk_col.unsqueeze(2).to_broadcast([P, HEADS, DK]), ALU.mult)
                V.tensor_tensor(qd_T[:], src, dq[:], ALU.mult).then_inc(qT_ready, 1)

            def decay_scores(j):
                dve.wait_ge(sc_done, j + 1)
                V.tensor_tensor(s_T[:], bank[6][:].rearrange("p (h c) -> p h c", h=HEADS), dmask[:],
                                ALU.mult).then_inc(sT_ready, 1)

            def gate_outputs(j):
                dve.wait_ge(out_done, j + 1)
                o = [bank[4 + h // 2][:, (h % 2) * DV:(h % 2 + 1) * DV] for h in range(HEADS)]
                for h in range(HEADS):
                    m1 = own.mark(V.bn_stats(bn[:, h, :], o[h]))
                own.wait(m1)
                for h in range(HEADS):
                    m1 = own.mark(V.bn_aggr(mv[:, j, h, :], bn[:, h, :]))
                own.wait(m1)
                for h in range(HEADS):
                    gh = g[:, j, h * DV:(h + 1) * DV]
                    ins = V.scalar_tensor_tensor(gh, o[h], mv[:, j, h, 0:1], gh, ALU.subtract, ALU.mult)
                ins.then_inc(out_used, 1)
                if j < TT - 1:
                    dve.wait_ge(st_done, j + 1)
                    for h in range(HEADS):
                        inc = bank[6 + h // 2][:, (h % 2) * DV:(h % 2 + 1) * DV]
                        if j == 0:
                            ins = V.tensor_copy(state[:, h, :], inc)
                        else:
                            ins = V.scalar_tensor_tensor(state[:, h, :], state[:, h, :], CHUNK_DECAY[h], inc,
                                                         ALU.mult, ALU.add)
                    ins.then_inc(state_ready, 1)

            behind = {(10, 3): (turned_qk, 0), (11, 0): (decay_scores, 0), (11, 1): (gate_outputs, 0),
                      (11, 2): (turned_qk, 1), (11, 3): (decay_scores, 1), (12, 0): (gate_outputs, 1),
                      (12, 1): (turned_qk, 2), (12, 2): (decay_scores, 2), (12, 3): (gate_outputs, 2),
                      (13, 0): (turned_qk, 3), (13, 1): (decay_scores, 3), (13, 2): (gate_outputs, 3)}

            for c in range(1, CHUNKS):
                for s in range(4):
                    if s == 3:
                        evac(c - 1)
                    lo_part(c, s)
                    for ct in RET_TURNED.get((c, s), ()):
                        turned_lo_part(CT + ct, CT + ct + 1, r_hi, r_lo, PR_GN, ct)
                    if c == 1 and s == 0:
                        dve.wait_ge(bexp_done, 1)
                        V.tensor_copy(bexp[:], bank[4][:].rearrange("p (m e) -> p e m", e=NE)).then_inc(bexp_ready, 1)
                    if c == 6:
                        rotate(V, own, q, 0, s, rot_a, rot_b, q_ready, dve)
                    steps = CONV_START if (c, s) == (2, 3) else CONV_STEPS.get(c, 0)
                    conv(conv_steps[:steps])
                    conv_steps = conv_steps[steps:]
                    if (c, s) in ((14, 3), (15, 0)):
                        dve.wait_ge(ln_mean, 1)
                        first = 0 if c == 14 else CT // 2
                        for ct in range(first, first + CT // 2):
                            V.scalar_tensor_tensor(cv[:, ct, :], bank[4][:], -1.0 / D, cv[:, ct, :],
                                                   ALU.mult, ALU.add).then_inc(ln_cent, 1)
                    if (c, s) == (15, 3):
                        dve.wait_ge(ln_dev, 1)
                        V.reciprocal(lrs[:], lrs[:]).then_inc(ln_rs, 1)
                    for i in LN_STEPS.get((c, s), ()):
                        if i < CT:
                            dve.wait_ge(ln_scaled, i + 1)
                            V.tensor_scalar(cv[:, i, :], cv[:, i, :], col(PR_LNW, i), col(PR_LNB, i),
                                            ALU.mult, ALU.add).then_inc(ln_z, 1)
                        if 1 <= i <= CT:
                            dve.wait_ge(ln_sig, i)
                            V.tensor_tensor(cv[:, i - 1, :], cv[:, i - 1, :], lsg[(i - 1) % 2][:],
                                            ALU.mult).then_inc(ln_val, 1)
                        if i >= 2:
                            dve.wait_ge(ln_hi, i - 1)
                            V.tensor_tensor(c_lo[:, i - 2, :], cv[:, i - 2, :], c_hi[:, i - 2, :].bitcast(F32),
                                            ALU.subtract).then_inc(c_ready, 1)
                    if (c, s) in behind:
                        f, j = behind[c, s]
                        f(j)
                if c == 13:
                    dve.wait_ge(dev_ready, 1)
                    own.link(V.reciprocal(mv[:, :, :, 1], mv[:, :, :, 1]))
                    for j in range(TT):
                        gj = g[:, j, :].rearrange("p (h d) -> p h d", h=HEADS)
                        ins = V.tensor_tensor(gj, gj, mv[:, j, :, 1:2].to_broadcast([P, HEADS, DV]), ALU.mult)
                    ins.then_inc(gated, 1)
            evac(CHUNKS - 1)

            inverse_rms(1, 0, TT)
            dve.wait_ge(lg_done, 1)
            for tt in range(TT):
                ins = V.scalar_tensor_tensor(lg[:, tt, :], bank[0][:, tt * NE:(tt + 1) * NE], ss[:, tt:tt + 1],
                                             b_rout[:], ALU.mult, ALU.add)
            own.link(ins)
            marks = [own.mark(V.max(top[:, tt, :], lg[:, tt, :])) for tt in range(TT)]
            for tt in range(TT):
                own.wait(marks[tt])
                ins = V.max_index(topi[:, tt, :], top[:, tt, :], lg[:, tt, :])
            own.link(ins)
            V.tensor_scalar(nmax, top[:, :, 0], -1.0, None, ALU.mult).then_inc(lg_ready, 1)
            own.link(V.tensor_copy(topf[:], topi[:, :, 0:TOPK]))
            hot = [P, TT, TOPK, NE]
            own.link(V.tensor_tensor(oh[:], iota_e.unsqueeze(1).unsqueeze(1).to_broadcast(hot),
                                     topf[:].unsqueeze(3).to_broadcast(hot), ALU.is_equal))
            V.tensor_reduce(msk[:], oh[:].rearrange("p t k e -> p t e k"), AX_X, ALU.add).then_inc(msk_ready, 1)
            for w in range(2):
                V.tensor_tensor(ohb[:, :, :, w, :], oh[:], ids[:, w].unsqueeze(3).to_broadcast(hot), ALU.mult)
            for tt in range(TT):
                V.tensor_scalar(xn2[:, tt, :], x[:, tt, :], ss[:, tt:tt + 1], None, ALU.mult).then_inc(xn_ready, 1)
            dve.wait_ge(rank_done, 1)
            V.tensor_reduce(maxc[:], bank[1][0:1, TT * NE:(TT + 1) * NE], AX_X, ALU.max).then_inc(maxc_ready, 1)
            own.link(V.tensor_tensor(prod[:], oh[:], bank[1][:, 0:TT * NE].rearrange("p (t e) -> p t e", e=NE)
                                     .unsqueeze(2).to_broadcast(hot), ALU.mult))
            own.link(V.tensor_reduce(rank, prod[:], AX_X, ALU.add))

            def slot_tables(m, chain):
                caps = [P, TT * TOPK, CAP]
                V.tensor_tensor(oha[:].rearrange("p t k c -> p (t k) c"), iota_cap.unsqueeze(1).to_broadcast(caps),
                                rank.rearrange("p t k -> p (t k)").unsqueeze(2).to_broadcast(caps),
                                ALU.is_equal).then_inc(oh_ready, 1)
                dve.wait_ge(oh_ready, m + 1)
                chain.link(V.tensor_scalar(rank, rank, -float(CAP), None, ALU.add))
                dve.wait_ge(tab_done, m + 1)
                V.tensor_scalar(tok_tab[0:CAP, 0:NE], bank[4][0:CAP, NE:2 * NE], float(EMPTY), None, ALU.add)
                V.tensor_scalar(asg_tab[0:CAP, 0:NE], bank[4][0:CAP, 0:NE], float(EMPTY), None,
                                ALU.add).then_inc(tab_ready, 1)

            slot_tables(0, own)
            dve.wait_ge(exp_ready, TT)
            own.link(V.tensor_reduce(wsum, wtop, AX_X, ALU.add))
            own.link(V.reciprocal(wsum, wsum))
            own.link(V.tensor_tensor(wtop, wtop, wsum.unsqueeze(2).to_broadcast([P, TT, TOPK]), ALU.mult))

            def turned_x(c, j):
                dve.wait_ge(xt_done, 2 * c + j + 3)
                V.tensor_tensor(x_T[:, 4 * j:4 * j + 4, :], bank[6 + j][:, 0:4 * CAP].rearrange("p (k c) -> p k c", c=CAP),
                                par[:, PR_FFN + 4 * j:PR_FFN + 4 * j + 4].unsqueeze(2).to_broadcast([P, 4, CAP]),
                                ALU.mult).then_inc(xT_ready, 1)

            LINKS = 12

            def split_down(n, r):
                dve.wait_ge(dn_hi_ready, 4 * n + r + 1)
                V.tensor_tensor(dn_lo[r][:], wslot[GU_SLOTS + r][:], dn_hi[r][:].bitcast(F32),
                                ALU.subtract).then_inc(dn_lo_ready, 1)

            def expert(n, c, e):
                chain = Chain(dve, dve_moe, n * LINKS)
                bias = bexp[:, bass.ds(e, 1), :]
                for r in range(4):
                    split_down(n, r)
                for i in range(5):
                    if i < 4:
                        zb = z[i % 2]
                        dve.wait_ge(act_ready, 4 * n + i + 1)
                        dve.wait_ge(gu_done, 4 * n + i + 1)
                        for half in range(2):
                            bb = bias[:, :, CT * half + 2 * i:CT * half + 2 * i + 2].rearrange("p o i -> p (o i)")
                            ins = V.tensor_tensor(zb[:, half], bank[i][:, half * 2 * CAP:(half + 1) * 2 * CAP]
                                                  .rearrange("p (i c) -> p i c", c=CAP),
                                                  bb.unsqueeze(2).to_broadcast([P, 2, CAP]), ALU.add)
                        chain.link(ins)
                        V.tensor_scalar(zb[:], zb[:], LIMIT, None, ALU.min).then_inc(z_ready, 1)
                        dve.wait_ge(z_ready, 4 * n + i + 1)
                        chain.link(V.tensor_scalar(zb[:, 1], zb[:, 1], -LIMIT, 1.0, ALU.max, ALU.add))
                        chain.link(V.tensor_tensor(gu[i % 2][:], zb[:, 0], zb[:, 1], ALU.mult))
                    if i >= 1:
                        b = i - 1
                        dve.wait_ge(sg_ready, 4 * n + b + 1)
                        V.tensor_tensor(act_T[:, 2 * b:2 * b + 2, :], gu[b % 2][:], sg[b % 2][:],
                                        ALU.mult).then_inc(act_ready, 1)
                        dve.wait_ge(act_hi_ready, 4 * n + b + 1)
                        V.tensor_tensor(act_lo[:, 2 * b:2 * b + 2, :], act_T[:, 2 * b:2 * b + 2, :],
                                        act_hi[:, 2 * b:2 * b + 2, :].bitcast(F32), ALU.subtract) \
                            .then_inc(act_lo_ready, 1)
                assert chain.n == LINKS
                for j in range(2):
                    turned_x(c + 1, j)

            for j in range(2):
                turned_x(0, j)
            own.link(V.tensor_tensor(prod[:], oh[:], wtop.unsqueeze(3).to_broadcast(hot), ALU.mult))
            V.tensor_reduce(wexp[:], prod[:].rearrange("p t k e -> p t e k"), AX_X, ALU.add).then_inc(wexp_ready, 1)
            with dve.Fori(0, NE) as e:
                expert(e, e, e)
            dve.wait_ge(maxc_ready, 1)
            fullest = dve.value_load(maxc[0:1, 0:1], min_val=0, max_val=T)
            with dve.If(fullest > CAP):
                with dve.Fori(1, PASSES) as m:
                    with dve.If(fullest > m * CAP):
                        dve.wait_ge(pass_done, m)
                        slot_tables(m, Chain(dve, dve_pass, m - 1))
                        for j in range(2):
                            turned_x(m * (NE + 1), j)
                        with dve.Fori(0, NE) as e:
                            expert(m * NE + e, m * (NE + 1) + e, e)

            dve.wait_ge(wT_done, 1)
            V.tensor_copy(wexp_T[:], bank[6][0:NE, :]).then_inc(wT_ready, 1)

            def split_gate(kt):
                s, kk = kt // 2, kt % 2
                dve.wait_ge(pg_hi_ready, kt + 1)
                V.scalar_tensor_tensor(pg_lo[s][:, kk, :], pg_raw[s][:, kk, :], col(PR_PLE, kt),
                                       pg_hi[s][:, kk, :].bitcast(F32), ALU.mult, ALU.subtract).then_inc(pg_lo_ready, 1)

            def split_x(tt, j):
                dve.wait_ge(x_hi_ready, 2 * tt + j + 1)
                V.tensor_tensor(x_lo[:, tt, 4 * j:4 * j + 4, :], bank[4 + 2 * (tt % 2) + j][:]
                                .rearrange("p (c t) -> p c t", t=P), x_hi[:, tt, 4 * j:4 * j + 4, :].bitcast(F32),
                                ALU.subtract).then_inc(x_lo_ready, 1)

            def finish(group, first, last):
                inverse_rms(group, TT + first, TT + last)
                for tt in range(first, last):
                    V.scalar_tensor_tensor(x[:, tt, :], x[:, tt, :], ss[:, TT + tt:TT + tt + 1], g_fin[:],
                                           ALU.mult, ALU.mult).then_inc(fin_ready, 1)

            def add_biases(tt):
                for i in (2 * tt, 2 * tt + 1):
                    dve.wait_ge(bias_done, i + 1)
                    xs = x[:, tt, (i % 2) * NCOL:(i % 2 + 1) * NCOL]
                    own.mark(V.tensor_tensor(xs, bank[(i + 4) % 8][:], xs, ALU.add))
                return own.n

            for kt in range(6):
                split_gate(kt)
            def add_experts(tt, added):
                dve.wait_ge(yb_in[tt], 16)
                own.wait(added)
                for kk in range(TOPK):
                    ins = V.scalar_tensor_tensor(x[:, tt, :], yb[tt % 3][:, kk, :], wtop[:, tt, kk:kk + 1],
                                                 x[:, tt, :], ALU.mult, ALU.add)
                    if kk < TOPK - 1:
                        own.link(ins)
                ins.then_inc(x2_ready, 1)

            def split_tile(tt):
                for j in range(2):
                    split_x(tt, j)

            def inverse_gate_rms(group, first, last):
                inverse_rms(group, first, last)
                dve.sem_inc(inv_ready, 1)

            def add_gated(tt):
                for n2 in range(2):
                    i = 2 * tt + n2
                    xs = x[:, tt, n2 * NCOL:(n2 + 1) * NCOL]
                    dve.wait_ge(gate_ready, i + 1)
                    V.tensor_tensor(gate[n2][:], gate[n2][:], pp[:, tt, n2 * NCOL:(n2 + 1) * NCOL],
                                    ALU.mult).then_inc(gate_used, 1)
                    dve.wait_ge(gate_used, i + 1)
                    V.tensor_tensor(xs, xs, gate[n2][:], ALU.add).then_inc(x3_ready, 1)

            add_experts(0, add_biases(0))
            added2 = add_biases(2)
            split_tile(0)
            for kt in (6, 7):
                split_gate(kt)
            add_experts(1, add_biases(1))
            added3 = add_biases(3)
            split_tile(1)
            inverse_gate_rms(2, 0, 2)
            add_experts(2, added2)
            split_tile(2)
            add_gated(0)
            add_experts(3, added3)
            split_tile(3)
            inverse_gate_rms(3, 2, TT)
            add_gated(1)
            add_gated(2)
            dve.wait_ge(g_fin_in, 16)
            finish(4, 0, 2)
            add_gated(3)
            finish(5, 2, TT)


def constants():
    import numpy as np
    f = np.float32
    token = np.arange(T, dtype=f)
    inv_freq = (f(10000.0) ** (-np.arange(HALF, dtype=f) / f(HALF))).astype(f)
    ang = (token[:, None] * inv_freq[None, :]).astype(f)
    cos, sin, scale = np.cos(ang), np.sin(ang), f(DK ** -0.5)
    rope = np.stack([cos, sin, cos * scale, sin * scale]).reshape(4, TT, P, HALF).transpose(2, 0, 1, 3)
    log_gamma = np.log1p(-np.exp2(-5.0 - np.arange(HEADS)))
    i = np.arange(P)
    rel = i[None, :] - i[:, None]
    dmask = np.where(rel[:, None, :] >= 0, np.exp(log_gamma[None, :, None] * np.maximum(rel, 0)[:, None, :]), 0.0)
    dq = np.broadcast_to(np.exp(log_gamma[:, None] * (i + 1.0))[None], (P, HEADS, P))
    cst = np.zeros((P, 168))
    cst[:, 0:CAP] = np.arange(CAP)
    cst[:, 96:128] = np.arange(NE)
    tok = np.arange(TT)[None, :, None] * P + i[:, None, None]
    cst[:, 128:144] = (tok * TOPK + np.arange(TOPK) - EMPTY).reshape(P, 16)
    cst[:, 144:160] = np.broadcast_to(tok - EMPTY, (P, TT, TOPK)).reshape(P, 16)
    cst[:, 164] = EPS
    cst[:, 160:164] = np.exp(log_gamma[None, :] * (P - 1.0 - i[:, None]))
    out = dict(ident=np.eye(P), tri=(i[:, None] < i[None, :]), cst=cst, rope=rope.reshape(P, -1),
               dmask=dmask.reshape(P, -1), dq=dq.reshape(P, -1))
    return {n: np.ascontiguousarray(a.astype(f)) for n, a in out.items()}


_INS = ["x", "p", "g_mix", "w_in", "ret_gn_w", "w_ret_out", "w_dw", "b_dw", "conv_ln_w", "conv_ln_b", "w_conv_out",
        "b_conv_out", "w_o", "g_ffn", "w_router", "b_router", "w_gu", "b_gu", "w_down", "b_down", "g_ple",
        "w_ple_gate", "w_ple_proj", "g_final"]


def kernel(**inputs):
    import types

    import numpy as np
    import concourse.bacc as bacc
    from concourse.bass_utils import run_bass_kernel_spmd

    nc = bacc.Bacc("TRN2", target_bir_lowering=False, num_devices=1)
    arrays, views = {}, {}
    for name in _INS:
        a = np.ascontiguousarray(inputs[name])
        if name == "x":
            a = a.reshape(T, D)
        elif name == "p":
            a = a.reshape(T, PLE)
        elif name != "g_final":
            a = a.reshape(a.shape[1:])
        arrays["in_" + name] = a
        views[name] = nc.dram_tensor("in_" + name, a.shape, F32, kind="ExternalInput").ap()
    for name, a in constants().items():
        arrays["const_" + name] = a
        views[name] = nc.dram_tensor("const_" + name, a.shape, F32, kind="ExternalInput").ap()
    views["out"] = nc.dram_tensor("out", (T, D), F32, kind="ExternalOutput").ap()
    build_layer(nc, types.SimpleNamespace(**views))
    r = run_bass_kernel_spmd(nc, [arrays], core_ids=[0])
    return r.results[0]["out"].reshape(1, T, D)
```
